# Optimizing a Trainium2 kernel written in Bass

```python
import math
import jax, jax.numpy as jnp
from jax import lax
import numpy as np

D_MODEL = 1024
BATCH = 1
SEQ = 512
DEPTH = 2

HEAD_DIM = 64
HEADS_A = 8
VDIM_A = 2 * HEAD_DIM
WIDTH_A = HEADS_A * VDIM_A
DILATED_GROUPS = ((128, 1), (512, 4), (2048, 16))
N_GROUPS_B = 3
HEADS_PER_GROUP_B = 4
HEADS_B = N_GROUPS_B * HEADS_PER_GROUP_B
WIDTH_B = HEADS_PER_GROUP_B * HEAD_DIM
D_FF = 4 * D_MODEL
ROPE_THETA = 500000.0
ROT_FRACTION = 4
Q_BLOCK = 128
EPS = 1e-6
NEG_INF = -1e30
Q_A_COLS = HEADS_A * 2 * HEAD_DIM
K_A_COLS = HEADS_A * 2 * HEAD_DIM
V_A_COLS = HEADS_A * VDIM_A
QKV_B_COLS = HEADS_B * HEAD_DIM
GATE_COLS = 2 * D_MODEL
IN_COLS = Q_A_COLS + K_A_COLS + V_A_COLS + 3 * QKV_B_COLS + GATE_COLS
IN_SPLITS = (
    Q_A_COLS,
    Q_A_COLS + K_A_COLS,
    Q_A_COLS + K_A_COLS + V_A_COLS,
    Q_A_COLS + K_A_COLS + V_A_COLS + QKV_B_COLS,
    Q_A_COLS + K_A_COLS + V_A_COLS + 2 * QKV_B_COLS,
    Q_A_COLS + K_A_COLS + V_A_COLS + 3 * QKV_B_COLS,
)


def rms_norm(x, g):
    xf = x.astype(jnp.float32)
    y = xf * lax.rsqrt(jnp.mean(xf * xf, axis=-1, keepdims=True) + EPS)
    return (y * g.astype(jnp.float32)).astype(x.dtype)

def rope_tables(positions):
    rot = HEAD_DIM // ROT_FRACTION
    inv_freq = ROPE_THETA ** (-jnp.arange(0, rot, 2, dtype=jnp.float32) / rot)
    ang = positions.astype(jnp.float32)[..., None] * inv_freq
    return jnp.cos(ang), jnp.sin(ang)

def apply_rope(x, cos, sin):
    half = cos.shape[-1]
    bshape = cos.shape[:2] + (1,) * (x.ndim - 3) + (half,)
    cs = cos.reshape(bshape).astype(x.dtype)
    sn = sin.reshape(bshape).astype(x.dtype)
    x1, x2, rest = x[..., :half], x[..., half:2 * half], x[..., 2 * half:]
    return jnp.concatenate([x1 * cs - x2 * sn, x2 * cs + x1 * sn, rest], axis=-1)

def diff_attention(q, k, v, lam):
    b, s, h, _, dh = q.shape
    nq = s // Q_BLOCK
    scale = dh ** -0.5
    qb = q.reshape(b, nq, Q_BLOCK, h, 2, dh).transpose(1, 0, 3, 4, 2, 5)
    kt = k.transpose(0, 2, 3, 1, 4)
    vt = v.transpose(0, 2, 1, 3)

    def block(qblk):
        sc = jnp.einsum('bhcqd,bhckd->bhcqk', qblk, kt).astype(jnp.float32) * scale
        p = jax.nn.softmax(sc, axis=-1)
        w = p[:, :, 0] - lam * p[:, :, 1]
        return jnp.einsum('bhqk,bhkd->bhqd', w.astype(vt.dtype), vt)

    o = lax.map(block, qb)
    return o.transpose(1, 0, 3, 2, 4).reshape(b, s, h, 2 * dh)

def dilated_window_attention(q, k, v, dilation, side):
    b, s, h, dh = q.shape
    L = s // dilation
    nb = -(-L // side)
    Lp = nb * side

    def split(t):
        return t.reshape(b, L, dilation, h, dh).transpose(0, 2, 3, 1, 4)

    qs = jnp.pad(split(q), ((0, 0),) * 3 + ((0, Lp - L), (0, 0)))
    pad_kv = ((0, 0),) * 3 + ((side, Lp - L + side), (0, 0))
    kp = jnp.pad(split(k), pad_kv)
    vp = jnp.pad(split(v), pad_kv)

    def band(t):
        return jnp.concatenate(
            [t[..., j * side:j * side + Lp, :].reshape(b, dilation, h, nb, side, dh) for j in range(3)],
            axis=-2)

    kb, vb = band(kp), band(vp)
    qb = qs.reshape(b, dilation, h, nb, side, dh)
    sc = jnp.einsum('bghnqd,bghnkd->bghnqk', qb, kb).astype(jnp.float32) * (dh ** -0.5)
    blk = jnp.arange(nb)[:, None, None]
    qpos = blk * side + jnp.arange(side)[None, :, None]
    kpos = blk * side - side + jnp.arange(3 * side)[None, None, :]
    valid = (jnp.abs(qpos - kpos) <= side) & (kpos >= 0) & (kpos < L)
    sc = jnp.where(valid, sc, NEG_INF)
    lse = jax.nn.logsumexp(sc, axis=-1)
    p = jnp.exp(sc - lse[..., None])
    o = jnp.einsum('bghnqk,bghnkd->bghnqd', p.astype(v.dtype), vb)
    o = o.reshape(b, dilation, h, Lp, dh)[..., :L, :].transpose(0, 3, 1, 2, 4).reshape(b, s, h, dh)
    lse = lse.reshape(b, dilation, h, Lp)[..., :L].transpose(0, 3, 1, 2).reshape(b, s, h)
    return o, lse

def first_inputs(seed: int = 0) -> dict:
    key = jax.random.key(seed)
    ks = jax.random.split(key, 20)
    D = D_MODEL
    nrm = lambda k, shape, s: jax.random.normal(k, shape, jnp.float32) * s
    x = nrm(ks[0], (BATCH, SEQ, D), 1.0)
    c = nrm(ks[1], (BATCH, D), 1.0)
    offsets = jax.random.randint(ks[2], (BATCH, 1), 0, 1024, dtype=jnp.int32)
    positions = (jnp.arange(SEQ, dtype=jnp.int32)[None, :] + offsets).astype(jnp.int32)
    return {
        "x": x,
        "c": c,
        "positions": positions,
        "ada_w": nrm(ks[3], (DEPTH, D, 6 * D), D ** -0.5),
        "ada_b": nrm(ks[4], (DEPTH, 6 * D), 0.02),
        "norm_mix_g": 1.0 + nrm(ks[5], (DEPTH, D), 0.02),
        "norm_mlp_g": 1.0 + nrm(ks[6], (DEPTH, D), 0.02),
        "w_in": nrm(ks[7], (DEPTH, D, IN_COLS), D ** -0.5),
        "qk_gain_a": 1.0 + nrm(ks[8], (DEPTH, 2, HEAD_DIM), 0.02),
        "lambda_a": nrm(ks[9], (DEPTH, 4, HEAD_DIM), 0.1),
        "subln_g_a": 1.0 + nrm(ks[10], (DEPTH, VDIM_A), 0.02),
        "qk_gain_b": 1.0 + nrm(ks[11], (DEPTH, 2, HEAD_DIM), 0.02),
        "w_branch_a": nrm(ks[12], (DEPTH, WIDTH_A, D), WIDTH_A ** -0.5),
        "w_branch_b": nrm(ks[13], (DEPTH, WIDTH_B, D), WIDTH_B ** -0.5),
        "gate_bias": nrm(ks[14], (DEPTH, GATE_COLS), 0.02),
        "w_out": nrm(ks[15], (DEPTH, D, D), D ** -0.5),
        "w_mlp_up": nrm(ks[16], (DEPTH, D, D_FF), D ** -0.5),
        "w_mlp_down": nrm(ks[17], (DEPTH, D_FF, D), D_FF ** -0.5),
    }

def first_block(x, c, positions, ada_w, ada_b, norm_mix_g, norm_mlp_g, w_in, qk_gain_a,
              lambda_a, subln_g_a, qk_gain_b, w_branch_a, w_branch_b, gate_bias, w_out,
              w_mlp_up, w_mlp_down):
    b, s, _ = x.shape
    cos, sin = rope_tables(positions)
    cond = jax.nn.silu(c)
    for l in range(DEPTH):
        mod = (cond @ ada_w[l] + ada_b[l])[:, None, :]
        shift_m, scale_m, gate_m, shift_f, scale_f, gate_f = jnp.split(mod, 6, axis=-1)

        h = rms_norm(x, norm_mix_g[l]) * (1.0 + scale_m) + shift_m
        proj = h @ w_in[l]
        qa, ka, va, qb, kb, vb, gates = jnp.split(proj, IN_SPLITS, axis=-1)

        qa = apply_rope(rms_norm(qa.reshape(b, s, HEADS_A, 2, HEAD_DIM), qk_gain_a[l, 0]), cos, sin)
        ka = apply_rope(rms_norm(ka.reshape(b, s, HEADS_A, 2, HEAD_DIM), qk_gain_a[l, 1]), cos, sin)
        va = va.reshape(b, s, HEADS_A, VDIM_A)
        lam_init = 0.8 - 0.6 * math.exp(-0.3 * l)
        lv = lambda_a[l].astype(jnp.float32)
        lam = jnp.exp(jnp.sum(lv[0] * lv[1])) - jnp.exp(jnp.sum(lv[2] * lv[3])) + lam_init
        oa = diff_attention(qa, ka, va, lam)
        oa = (rms_norm(oa, subln_g_a[l]) * (1.0 - lam_init)).reshape(b, s, WIDTH_A)

        qb = apply_rope(rms_norm(qb.reshape(b, s, N_GROUPS_B, HEADS_PER_GROUP_B, HEAD_DIM), qk_gain_b[l, 0]), cos, sin)
        kb = apply_rope(rms_norm(kb.reshape(b, s, N_GROUPS_B, HEADS_PER_GROUP_B, HEAD_DIM), qk_gain_b[l, 1]), cos, sin)
        vb = vb.reshape(b, s, N_GROUPS_B, HEADS_PER_GROUP_B, HEAD_DIM)
        outs, lses = [], []
        for g, (window, dilation) in enumerate(DILATED_GROUPS):
            o_g, lse_g = dilated_window_attention(qb[:, :, g], kb[:, :, g], vb[:, :, g],
                                                  dilation, window // (2 * dilation))
            outs.append(o_g)
            lses.append(lse_g)
        wgt = jax.nn.softmax(jnp.stack(lses, axis=0), axis=0)
        ob = jnp.sum(wgt[..., None].astype(x.dtype) * jnp.stack(outs, axis=0), axis=0)
        ob = ob.reshape(b, s, WIDTH_B)

        g_a, g_b = jnp.split(jax.nn.sigmoid(gates + gate_bias[l]), 2, axis=-1)
        y = (g_a * (oa @ w_branch_a[l]) + g_b * (ob @ w_branch_b[l])) @ w_out[l]
        x = x + gate_m * y

        h = rms_norm(x, norm_mlp_g[l]) * (1.0 + scale_f) + shift_f
        x = x + gate_f * (jnp.square(jax.nn.relu(h @ w_mlp_up[l])) @ w_mlp_down[l])
    return x


DEPTH_2 = 1

GRID_W = 64
CTX_LEN = 256
N_MOD = 6
MLA_HEADS = 4
MLA_Q_RANK = 256
MLA_KV_RANK = 128
MLA_NOPE = 128
MLA_ROPE = 64
MLA_V = 128
MLA_QK = MLA_NOPE + MLA_ROPE
ROPE_AXIS = MLA_ROPE // 2
ROPE_BASE = 10000.0
ML_HEADS = 4
ML_QK = 64
ML_V = 128
ML_CHUNK = 64
CONV_W = 3
FGATE_BIAS_LO = 3.0
FGATE_BIAS_HI = 6.0
MLA_COLS = MLA_Q_RANK + MLA_KV_RANK + MLA_ROPE
ML_COLS = 2 * ML_HEADS * ML_QK + 2 * ML_HEADS * ML_V + 4 * ML_HEADS
IN_COLS_2 = MLA_COLS + ML_COLS
MIX_WIDTH = MLA_HEADS * MLA_V + ML_HEADS * ML_V
PEER_HEADS = 8
N_KEYS = 128
N_EXPERTS = N_KEYS * N_KEYS
PEER_DK = 256
PEER_DKH = PEER_DK // 2
PEER_TOPK = 16
PEER_BLOCK = 128


def rmsnorm(x, g):
    xf = x.astype(jnp.float32)
    y = xf * lax.rsqrt(jnp.mean(xf * xf, axis=-1, keepdims=True) + EPS)
    return (y * g.astype(jnp.float32)).astype(x.dtype)

def rope_tables_2(rows):
    row = jnp.repeat(jnp.arange(rows, dtype=jnp.float32), GRID_W)
    col = jnp.tile(jnp.arange(GRID_W, dtype=jnp.float32), rows)
    inv = ROPE_BASE ** (-jnp.arange(ROPE_AXIS // 2, dtype=jnp.float32) * (2.0 / ROPE_AXIS))
    ang_r = row[:, None] * inv
    ang_c = col[:, None] * inv
    return (jnp.cos(ang_r), jnp.sin(ang_r), jnp.cos(ang_c), jnp.sin(ang_c))

def rotate(t, cos, sin):
    half = t.shape[-1] // 2
    t1, t2 = t[..., :half], t[..., half:]
    cos = cos.astype(t.dtype)
    sin = sin.astype(t.dtype)
    return jnp.concatenate([t1 * cos - t2 * sin, t2 * cos + t1 * sin], axis=-1)

def apply_rope2d(t, rope):
    cos_r, sin_r, cos_c, sin_c = rope
    t_row = rotate(t[..., MLA_NOPE:MLA_NOPE + ROPE_AXIS], cos_r, sin_r)
    t_col = rotate(t[..., MLA_NOPE + ROPE_AXIS:], cos_c, sin_c)
    return jnp.concatenate([t[..., :MLA_NOPE], t_row, t_col], axis=-1)

def split_heads(t, n_heads):
    b, n, _ = t.shape
    return t.reshape(b, n, n_heads, -1).transpose(0, 2, 1, 3)

def merge_heads(t):
    b, h, n, d = t.shape
    return t.transpose(0, 2, 1, 3).reshape(b, n, h * d)

def mla_prep(cols, g_cq, w_uq, g_ckv, w_ukv, g_qn, g_kn, rope):
    b, n, _ = cols.shape
    c_q = cols[..., :MLA_Q_RANK]
    c_kv = cols[..., MLA_Q_RANK:MLA_Q_RANK + MLA_KV_RANK]
    k_rope = cols[..., MLA_Q_RANK + MLA_KV_RANK:]
    q = (rmsnorm(c_q, g_cq) @ w_uq).reshape(b, n, MLA_HEADS, MLA_QK)
    kv = (rmsnorm(c_kv, g_ckv) @ w_ukv).reshape(b, n, MLA_HEADS, MLA_NOPE + MLA_V)
    k = jnp.concatenate([kv[..., :MLA_NOPE],
                         jnp.broadcast_to(k_rope[:, :, None, :], (b, n, MLA_HEADS, MLA_ROPE))], axis=-1)
    v = kv[..., MLA_NOPE:].transpose(0, 2, 1, 3)
    q = rmsnorm(q, g_qn).transpose(0, 2, 1, 3)
    k = rmsnorm(k, g_kn).transpose(0, 2, 1, 3)
    if rope is not None:
        q = apply_rope2d(q, rope)
        k = apply_rope2d(k, rope)
    return q, k, v

def attend(q, k, v):
    s = jnp.einsum('bhqd,bhkd->bhqk', q, k).astype(jnp.float32) * (MLA_QK ** -0.5)
    p = jax.nn.softmax(s, axis=-1).astype(v.dtype)
    return jnp.einsum('bhqk,bhkd->bhqd', p, v)

def attend_blocked(q, k, v):
    b, h, n, dk = q.shape
    nb = n // Q_BLOCK
    qb = jnp.moveaxis(q.reshape(b, h, nb, Q_BLOCK, dk), 2, 0)
    ob = lax.map(lambda q_blk: attend(q_blk, k, v), qb)
    return jnp.moveaxis(ob, 0, 2).reshape(b, h, n, -1)

def mla_mixer(cols_lat, cols_ctx, g_cq, w_uq, g_ckv, w_ukv, g_qn, g_kn, rope, need_ctx_out):
    q_l, k_l, v_l = mla_prep(cols_lat, g_cq, w_uq, g_ckv, w_ukv, g_qn, g_kn, rope)
    q_c, k_c, v_c = mla_prep(cols_ctx, g_cq, w_uq, g_ckv, w_ukv, g_qn, g_kn, None)
    k_all = jnp.concatenate([k_c, k_l], axis=2)
    v_all = jnp.concatenate([v_c, v_l], axis=2)
    out_lat = merge_heads(attend_blocked(q_l, k_all, v_all))
    out_ctx = merge_heads(attend(q_c, k_c, v_c)) if need_ctx_out else None
    return out_lat, out_ctx

def centred_conv(u, w):
    k = w.shape[0]
    p = k // 2
    n = u.shape[1]
    up = jnp.pad(u, ((0, 0), (p, p), (0, 0)))
    return sum(up[:, j:j + n] * w[j] for j in range(k))

def mlstm_prep(cols, conv_w, b_i, b_f):
    b, n, _ = cols.shape
    n_qk = ML_HEADS * ML_QK
    n_v = ML_HEADS * ML_V
    qk = jax.nn.silu(centred_conv(cols[..., :2 * n_qk], conv_w))
    q = split_heads(qk[..., :n_qk], ML_HEADS).astype(jnp.float32) * (ML_QK ** -0.5)
    k = split_heads(qk[..., n_qk:], ML_HEADS).astype(jnp.float32)
    v = split_heads(cols[..., 2 * n_qk:2 * n_qk + n_v], ML_HEADS).astype(jnp.float32)
    o = cols[..., 2 * n_qk + n_v:2 * n_qk + 2 * n_v]
    gates = cols[..., 2 * n_qk + 2 * n_v:].astype(jnp.float32).reshape(b, n, 2, 2, ML_HEADS)
    ig = (gates[:, :, 0] + b_i.astype(jnp.float32)).transpose(2, 0, 3, 1)
    lf = jax.nn.log_sigmoid(gates[:, :, 1] + b_f.astype(jnp.float32)).transpose(2, 0, 3, 1)
    return q, k, v, o, ig, lf

def mlstm_scan(q, k, v, ig, lf, state, need_out):
    b, h, n_tok, _ = q.shape
    nc = n_tok // ML_CHUNK

    def chunks(a):
        return jnp.moveaxis(a.reshape(a.shape[:2] + (nc, ML_CHUNK) + a.shape[3:]), 2, 0)

    tri = jnp.tril(jnp.ones((ML_CHUNK, ML_CHUNK), dtype=bool))

    def body(carry, inp):
        c_mat, n_vec, m_prev = carry
        qc, kc, vc, ic, fc = inp
        cum_f = jnp.cumsum(fc, axis=-1)
        dmat = jnp.where(tri, cum_f[..., :, None] - cum_f[..., None, :] + ic[..., None, :], -jnp.inf)
        inter = cum_f + m_prev[..., None]
        m_t = jnp.maximum(inter, jnp.max(dmat, axis=-1))
        m_new = m_t[..., -1]
        w_s = jnp.exp(dmat[..., -1, :] - m_new[..., None])
        decay = jnp.exp(inter[..., -1] - m_new)
        c_new = decay[..., None, None] * c_mat + jnp.einsum('bhs,bhsv,bhsd->bhvd', w_s, vc, kc)
        n_new = decay[..., None] * n_vec + jnp.einsum('bhs,bhsd->bhd', w_s, kc)
        if not need_out:
            return (c_new, n_new, m_new), None
        wmat = jnp.exp(dmat - m_t[..., None]) * jnp.einsum('bhtd,bhsd->bhts', qc, kc)
        scale_inter = jnp.exp(inter - m_t)
        num = jnp.einsum('bhts,bhsv->bhtv', wmat, vc) + scale_inter[..., None] * jnp.einsum('bhvd,bhtd->bhtv', c_mat, qc)
        den = jnp.sum(wmat, axis=-1) + scale_inter * jnp.einsum('bhd,bhtd->bht', n_vec, qc)
        h_out = num / jnp.maximum(jnp.abs(den), jnp.exp(-m_t))[..., None]
        return (c_new, n_new, m_new), h_out

    state, hs = lax.scan(body, state, (chunks(q), chunks(k), chunks(v), chunks(ig), chunks(lf)))
    h_seq = jnp.moveaxis(hs, 0, 2).reshape(b, h, n_tok, -1) if need_out else None
    return state, h_seq

def mlstm_output(h_sum, o, g_out):
    b, h, n, dv = h_sum.shape
    hn = rmsnorm(h_sum.transpose(0, 2, 1, 3), g_out.reshape(h, dv)).reshape(b, n, h * dv)
    return (jax.nn.sigmoid(o.astype(jnp.float32)) * hn).astype(o.dtype)

def mlstm_mixer(cols_lat, cols_ctx, conv_w, b_i, b_f, g_out, need_ctx_out):
    q_l, k_l, v_l, o_l, ig_l, lf_l = mlstm_prep(cols_lat, conv_w, b_i, b_f)
    q_c, k_c, v_c, o_c, ig_c, lf_c = mlstm_prep(cols_ctx, conv_w, b_i, b_f)
    b = q_l.shape[0]
    outs_lat, outs_ctx = [], []
    for d in range(2):
        rev = d == 1

        def fl(a):
            return jnp.flip(a, axis=2) if rev else a

        state0 = (jnp.zeros((b, ML_HEADS, ML_V, ML_QK), jnp.float32),
                  jnp.zeros((b, ML_HEADS, ML_QK), jnp.float32),
                  jnp.zeros((b, ML_HEADS), jnp.float32))
        st_ctx, h_c = mlstm_scan(fl(q_c), fl(k_c), fl(v_c), fl(ig_c[d]), fl(lf_c[d]), state0, need_ctx_out)
        _, h_l = mlstm_scan(fl(q_l), fl(k_l), fl(v_l), fl(ig_l[d]), fl(lf_l[d]), st_ctx, True)
        outs_lat.append(fl(h_l))
        if need_ctx_out:
            outs_ctx.append(fl(h_c))
    out_lat = mlstm_output(outs_lat[0] + outs_lat[1], o_l, g_out)
    out_ctx = mlstm_output(outs_ctx[0] + outs_ctx[1], o_c, g_out) if need_ctx_out else None
    return out_lat, out_ctx

def peer(h, w_pq, sub_keys, expert_u, expert_v):
    b, n, d = h.shape
    xb_all = h.reshape(-1, PEER_BLOCK, d)

    def one(xb):
        q = (xb @ w_pq).reshape(PEER_BLOCK, PEER_HEADS, 2, PEER_DKH)
        s = jnp.einsum('thpd,hpkd->thpk', q, sub_keys).astype(jnp.float32)
        sv, si = lax.top_k(s, PEER_TOPK)
        cand = (sv[:, :, 0, :, None] + sv[:, :, 1, None, :]).reshape(PEER_BLOCK, PEER_HEADS, -1)
        cidx = (si[:, :, 0, :, None] * N_KEYS + si[:, :, 1, None, :]).reshape(PEER_BLOCK, PEER_HEADS, -1)
        best, pos = lax.top_k(cand, PEER_TOPK)
        eidx = jnp.take_along_axis(cidx, pos, axis=-1)
        g = jax.nn.softmax(best, axis=-1)
        act = jax.nn.gelu(jnp.einsum('thkd,td->thk', expert_u[eidx], xb).astype(jnp.float32), approximate=False)
        return jnp.einsum('thk,thkd->td', (g * act).astype(xb.dtype), expert_v[eidx])

    return lax.map(one, xb_all).reshape(b, n, d)

def second_inputs(seed: int = 0) -> dict:
    key = jax.random.key(seed)
    ks = jax.random.split(key, 24)

    def nrm(k, shape, s):
        return jax.random.normal(k, shape, jnp.float32) * s

    def gain(k, shape):
        return 1.0 + nrm(k, shape, 0.01)

    D, L = D_MODEL, DEPTH_2
    fgate = jnp.linspace(FGATE_BIAS_LO, FGATE_BIAS_HI, ML_HEADS, dtype=jnp.float32)
    return {
        'x': nrm(ks[0], (BATCH, SEQ, D), 1.0),
        'c': nrm(ks[1], (BATCH, D), 1.0),
        'ctx': nrm(ks[2], (BATCH, CTX_LEN, D), 1.0),
        'c_ctx': nrm(ks[3], (D,), 1.0),
        'w_ada': nrm(ks[4], (L, D, N_MOD * D), 0.5 * D ** -0.5),
        'b_ada': nrm(ks[5], (L, N_MOD * D), 0.01),
        'g_norm1': gain(ks[6], (L, D)),
        'w_in': nrm(ks[7], (L, D, IN_COLS_2), D ** -0.5),
        'g_cq': gain(ks[8], (L, MLA_Q_RANK)),
        'w_uq': nrm(ks[9], (L, MLA_Q_RANK, MLA_HEADS * MLA_QK), MLA_Q_RANK ** -0.5),
        'g_ckv': gain(ks[10], (L, MLA_KV_RANK)),
        'w_ukv': nrm(ks[11], (L, MLA_KV_RANK, MLA_HEADS * (MLA_NOPE + MLA_V)), MLA_KV_RANK ** -0.5),
        'g_qn': gain(ks[12], (L, MLA_QK)),
        'g_kn': gain(ks[13], (L, MLA_QK)),
        'conv_qk': nrm(ks[14], (L, CONV_W, 2 * ML_HEADS * ML_QK), CONV_W ** -0.5),
        'b_igate': nrm(ks[15], (L, 2, ML_HEADS), 0.01),
        'b_fgate': fgate[None, None, :] + nrm(ks[16], (L, 2, ML_HEADS), 0.01),
        'g_mlstm': gain(ks[17], (L, ML_HEADS * ML_V)),
        'w_out': nrm(ks[18], (L, MIX_WIDTH, D), MIX_WIDTH ** -0.5),
        'g_norm2': gain(ks[19], (L, D)),
        'w_pq': nrm(ks[20], (L, D, PEER_HEADS * PEER_DK), D ** -0.5),
        'sub_keys': nrm(ks[21], (L, PEER_HEADS, 2, N_KEYS, PEER_DKH), PEER_DKH ** -0.5),
        'expert_u': nrm(ks[22], (L, N_EXPERTS, D), D ** -0.5),
        'expert_v': nrm(ks[23], (L, N_EXPERTS, D), PEER_HEADS ** -0.5),
    }

def second_block(x, c, ctx, c_ctx, w_ada, b_ada, g_norm1, w_in, g_cq, w_uq, g_ckv, w_ukv, g_qn, g_kn,
              conv_qk, b_igate, b_fgate, g_mlstm, w_out, g_norm2, w_pq, sub_keys, expert_u, expert_v):
    n_lat = x.shape[1]
    ROWS = n_lat // GRID_W
    rope = rope_tables_2(ROWS)
    s_c = jax.nn.silu(c)
    s_cc = jax.nn.silu(c_ctx)
    for l in range(DEPTH_2):
        last = l == DEPTH_2 - 1
        mod_lat = (s_c @ w_ada[l] + b_ada[l])[:, None, :]
        mod_ctx = s_cc @ w_ada[l] + b_ada[l]
        sh1, sc1, gt1, sh2, sc2, gt2 = jnp.split(mod_lat, N_MOD, axis=-1)
        csh1, csc1, cgt1, csh2, csc2, cgt2 = jnp.split(mod_ctx, N_MOD, axis=-1)
        h_lat = rmsnorm(x, g_norm1[l]) * (1.0 + sc1) + sh1
        h_ctx = rmsnorm(ctx, g_norm1[l]) * (1.0 + csc1) + csh1
        cols_lat = h_lat @ w_in[l]
        cols_ctx = h_ctx @ w_in[l]
        mla_lat, mla_ctx = mla_mixer(cols_lat[..., :MLA_COLS], cols_ctx[..., :MLA_COLS],
                                     g_cq[l], w_uq[l], g_ckv[l], w_ukv[l], g_qn[l], g_kn[l], rope, not last)
        ml_lat, ml_ctx = mlstm_mixer(cols_lat[..., MLA_COLS:], cols_ctx[..., MLA_COLS:],
                                     conv_qk[l], b_igate[l], b_fgate[l], g_mlstm[l], not last)
        x = x + gt1 * (jnp.concatenate([mla_lat, ml_lat], axis=-1) @ w_out[l])
        h2 = rmsnorm(x, g_norm2[l]) * (1.0 + sc2) + sh2
        x = x + gt2 * peer(h2, w_pq[l], sub_keys[l], expert_u[l], expert_v[l])
        if not last:
            ctx = ctx + cgt1 * (jnp.concatenate([mla_ctx, ml_ctx], axis=-1) @ w_out[l])
            hc2 = rmsnorm(ctx, g_norm2[l]) * (1.0 + csc2) + csh2
            ctx = ctx + cgt2 * peer(hc2, w_pq[l], sub_keys[l], expert_u[l], expert_v[l])
    return x


def setup_inputs(seed=0):
    out = dict(first_inputs(seed))
    for name, value in second_inputs(seed + 1).items():
        if name != "x":
            out[name + "_2"] = value
    return out


def reference(
    x, c, positions, ada_w, ada_b, norm_mix_g, norm_mlp_g, w_in, qk_gain_a, lambda_a, subln_g_a,
    qk_gain_b, w_branch_a, w_branch_b, gate_bias, w_out, w_mlp_up, w_mlp_down, c_2, ctx_2,
    c_ctx_2, w_ada_2, b_ada_2, g_norm1_2, w_in_2, g_cq_2, w_uq_2, g_ckv_2, w_ukv_2, g_qn_2,
    g_kn_2, conv_qk_2, b_igate_2, b_fgate_2, g_mlstm_2, w_out_2, g_norm2_2, w_pq_2, sub_keys_2,
    expert_u_2, expert_v_2,
):
    x = first_block(
        x, c, positions, ada_w, ada_b, norm_mix_g, norm_mlp_g, w_in, qk_gain_a, lambda_a,
        subln_g_a, qk_gain_b, w_branch_a, w_branch_b, gate_bias, w_out, w_mlp_up, w_mlp_down,
    )
    return second_block(
        x, c_2, ctx_2, c_ctx_2, w_ada_2, b_ada_2, g_norm1_2, w_in_2, g_cq_2, w_uq_2, g_ckv_2,
        w_ukv_2, g_qn_2, g_kn_2, conv_qk_2, b_igate_2, b_fgate_2, g_mlstm_2, w_out_2, g_norm2_2,
        w_pq_2, sub_keys_2, expert_u_2, expert_v_2,
    )


_drawn_inputs = setup_inputs


def setup_inputs(seed=0):
    import zlib

    import numpy as np

    out = dict(_drawn_inputs(seed))
    spreads = {}
    factors = {'norm_mix_g': 8.0,
     'norm_mlp_g': 2.691,
     'qk_gain_a': 8.0,
     'lambda_a': 8.0,
     'subln_g_a': 8.0,
     'qk_gain_b': 8.0,
     'gate_bias': 8.0,
     'ctx_2': 6.885,
     'c_ctx_2': 3.566,
     'b_ada_2': 8.0,
     'g_norm1_2': 32.764,
     'g_cq_2': 47.748,
     'w_uq_2': 4.277,
     'g_ckv_2': 56.733,
     'g_qn_2': 42.21,
     'g_kn_2': 45.189,
     'conv_qk_2': 21.878,
     'b_igate_2': 64.0,
     'b_fgate_2': 4.682,
     'g_mlstm_2': 64.0,
     'g_norm2_2': 64.0}
    for name, (base, spread) in spreads.items():
        noise = np.random.default_rng([zlib.crc32(name.encode()), seed]).standard_normal(out[name].shape)
        drawn = base * np.exp(spread * noise) if base else spread * noise
        out[name] = __import__('jax').numpy.asarray(drawn.astype(out[name].dtype))
    for name, factor in factors.items():
        out[name] = (out[name] * factor).astype(out[name].dtype)
    return out
```

```python
from contextlib import ExitStack, contextmanager

import numpy as np

import concourse.bass as bass
from concourse import mybir

F32 = mybir.dt.float32
F32R = mybir.dt.float32r
I32 = mybir.dt.int32
U32 = mybir.dt.uint32
ACT = mybir.ActivationFunctionType
ALU = mybir.AluOpType
X = mybir.AxisListType.X

P = 128
D = 1024
KB = D // P
T = 512
TB = T // P
CTX = 256
TA = CTX + T
AB = TA // P
DEPTH = 2
HEADS_A = 8
FF = 4096
FB = FF // P
NEG = -1e30
LN_EXP = "natural_log_exp_and_others"
EPS = 1e-6
BANK = 512

COLS = {}
for _name, _n in (("ada_b", 48), ("g_mix", 8), ("g_mlp", 8), ("gate_bias", 16), ("gain_a", 2),
                  ("gain_b", 2), ("subln", 1), ("lam", 4), ("lam_init", 2)):
    _at = sum(n for _, n in COLS.values())
    COLS[_name] = (_at, _n)
NCOLS = sum(n for _, n in COLS.values())
COLS2 = {}
for _name, _n in (("ada_b", 48), ("g1", 8), ("g2", 8), ("c", 16), ("g_cq", 2), ("g_ckv", 1), ("g_qn", 2),
                  ("g_kn", 2), ("conv", 12), ("g_ml", 4)):
    _at = sum(n for _, n in COLS2.values())
    COLS2[_name] = (_at, _n)
NCOLS2 = sum(n for _, n in COLS2.values())

MLA_HEADS = 4
ML_HEADS = 4
HALF = TA // 2
PEER_HEADS = 8
TOPK = 16
NKEYS = 128
HI, LO = 0, 1
PASSES = ((HI, HI), (HI, LO), (LO, HI))


class Steps:

    def __init__(self, eng, done):
        self.eng, self.done, self.n = eng, done, 0

    def __call__(self, ins):
        ins.then_inc(self.done, 1)
        self.n += 1
        self.eng.wait_ge(self.done, self.n)

    def again(self):
        self.eng.sem_clear(self.done)
        self.n = 0

    def hold(self, met):
        self.eng.wait_ge(met, 1)


@contextmanager
def stage(nc, *names):
    with ExitStack() as ctx:
        sems = [ctx.enter_context(nc.semaphore(n)) for n in names]
        with nc.Block(no_gpsimd_drain=True) as block:
            yield (block, *sems)
        for s in sems:
            nc.sync.sem_clear(s)
        nc.all_engine_barrier(sem_only=True)


def bank(ps, i, n=BANK):
    return ps[:, i * BANK:i * BANK + n]


def refine(step, dve, y, sums, scale, work):
    step(dve.tensor_tensor(work, y, y, ALU.mult))
    step(dve.scalar_tensor_tensor(work, sums, EPS / scale, work, ALU.add, ALU.mult))
    step(dve.tensor_scalar(work, work, -0.5 * scale, 1.5, ALU.mult, ALU.add))
    step(dve.tensor_tensor(y, y, work, ALU.mult))



def ada_stage(nc, M, w_tiles, first, cond, n_cond, bias, out):
    TURNS = 6
    with stage(nc, *[f"landed{i}" for i in range(KB)], "tiles_done", "rows_taken", "turned", "act_done",
               "dve_done") as (block, *s):
        landed, (tiles_done, rows_taken, turned, act_done, dve_done) = s[:KB], s[KB:]
        rows, columns_bank = M.sq, 2

        @block.sync
        def _(sp):
            with sp.Fori(0, TURNS) as g:
                for k in range(KB):
                    sp.wait_ge(tiles_done, g * KB + (k + 1))
                    sp.dma_start(M.ring[:, k], w_tiles[first + g * KB + k]).then_inc(landed[k], 16)

        @block.tensor
        def _(pe):
            pe.sem_inc(tiles_done, KB)
            pe.sem_inc(turned, 1)
            with pe.Fori(0, TURNS) as g:
                for k in range(KB):
                    pe.wait_ge(landed[k], g * 16 + 16)
                    for b in range(2):
                        last = pe.matmul(bank(M.ps, b)[0:n_cond], cond[:, k], M.ring[:, k, b * BANK:(b + 1) * BANK],
                                         start=k == 0, stop=k == KB - 1)
                    last.then_inc(tiles_done, 1)
                pe.wait_ge(rows_taken, g * 2 + 2)
                for m in range(KB):
                    at = columns_bank * BANK + m * n_cond
                    last = pe.matmul(M.ps[:, at:at + n_cond], rows[0:n_cond, m // 4, m % 4 * P:(m % 4 + 1) * P],
                                     M.ident[0:n_cond, 0:n_cond], start=True, stop=True)
                last.then_inc(turned, 1)

        @block.scalar
        def _(act):
            step = Steps(act, act_done)
            with act.Fori(0, TURNS) as g:
                act.wait_ge(tiles_done, g * KB + 2 * KB)
                act.wait_ge(turned, g + 1)
                step(act.copy(rows[0:n_cond, 1], bank(M.ps, 1)[0:n_cond]))
                act.sem_inc(rows_taken, 1)
                step.again()

        @block.vector
        def _(dve):
            step = Steps(dve, dve_done)
            with dve.Fori(0, TURNS) as g:
                dve.wait_ge(tiles_done, g * KB + 2 * KB)
                dve.wait_ge(turned, g + 1)
                step(dve.tensor_copy(rows[0:n_cond, 0], bank(M.ps, 0)[0:n_cond]))
                dve.sem_inc(rows_taken, 1)
                dve.wait_ge(turned, g + 2)
                src = M.ps[:, columns_bank * BANK:columns_bank * BANK + KB * n_cond].rearrange(
                    "p (m c) -> p m c", c=n_cond)
                for c in range(n_cond):
                    step(dve.tensor_tensor(out[:, bass.ds(g * KB, KB), c], src[:, :, c],
                                           bias[:, bass.ds(g * KB, KB)], ALU.add))
                step.again()


def norm_part(nc, M, src, n, parts, g_col, scale_col, shift_col, dst, factor=1.0 / D):
    with stage(nc, "squares", "summed", "root", "act_done", "dve_done", "sq_used") as (
            block, squares, summed, root, act_done, dve_done, sq_used):
        @block.scalar
        def _(act):
            step = Steps(act, act_done)
            act.preload_act_table_set(LN_EXP)
            for k in range(parts):
                if k >= 2:
                    act.wait_ge(sq_used, k - 1)
                step(act.activation(M.sq[:, k % 2, 0:n], src(k), ACT.Square))
                act.sem_inc(squares, 1)
            act.wait_ge(sq_used, parts)
            step(act.activation(M.ln[:, 0:n], bank(M.ps, 0, n), ACT.Ln, bias=M.eps[:, 0:1], scale=factor))
            step(act.activation(M.rstd[:, 0:n], M.ln[:, 0:n], ACT.Exp, scale=-0.5))
            act.sem_inc(root, 1)

        @block.tensor
        def _(pe):
            for k in range(parts):
                pe.wait_ge(squares, k + 1)
                pe.matmul(bank(M.ps, 0, n), M.ones[:, :], M.sq[:, k % 2, 0:n], start=k == 0,
                          stop=k == parts - 1).then_inc(sq_used, 1)

        @block.vector
        def _(dve):
            step = Steps(dve, dve_done)
            step(dve.scalar_tensor_tensor(M.gs[:, 0:parts], scale_col, 1.0, g_col, ALU.add, ALU.mult))
            dve.wait_ge(root, 1)
            refine(step, dve, M.rstd[:, 0:n], bank(M.ps, 0, n), factor, M.tmp2[:, 0:n])
            for k in range(parts):
                step(dve.tensor_tensor(M.tmp[:, 0:n], src(k), M.rstd[:, 0:n], ALU.mult))
                o = dst(k)
                i = M.tmp[:, 0:n]
                if len(o.shape) == 3:
                    i = i.rearrange("p (r l) -> p r l", r=o.shape[1])
                step(dve.tensor_scalar(o, i, M.gs[:, k:k + 1], shift_col[:, k:k + 1], ALU.mult, ALU.add))


def residual_stage(nc, M, w_tiles, first, rhs, gate, natural):
    RING = 4
    with stage(nc, *[f"landed{i}" for i in range(RING)], "tiles_done", "added", "dve_done") as (block, *s):
        landed, (tiles_done, added, dve_done) = s[:RING], s[RING:]

        @block.sync
        def _(sp):
            with sp.Fori(0, KB // RING) as g:
                for j in range(RING):
                    sp.wait_ge(tiles_done, g * RING + (j + 1))
                    sp.dma_start(M.ring[:, j], w_tiles[first + g * RING + j]).then_inc(landed[j], 16)

        @block.tensor
        def _(pe):
            pe.sem_inc(tiles_done, RING)
            with pe.Fori(0, KB // RING) as g:
                for j in range(RING):
                    pe.wait_ge(landed[j], g * 16 + 16)
                    pe.wait_ge(added, g * RING + (j + 1))
                    for k in range(KB):
                        last = pe.matmul(bank(M.ps, j), M.ring[:, j, k * P:(k + 1) * P], rhs[:, k],
                                         start=k == 0, stop=k == KB - 1)
                    last.then_inc(tiles_done, 1)

        @block.vector
        def _(dve):
            step = Steps(dve, dve_done)
            dve.sem_inc(added, RING)
            with dve.Fori(0, KB // RING) as g:
                for j in range(RING):
                    dve.wait_ge(tiles_done, g * RING + (RING + j + 1))
                    m = g * RING + j
                    x_m, y_m = M.x[:, m], bank(M.ps, j)
                    if natural:
                        x_m = x_m.rearrange("p (r l) -> p r l", r=4)
                        y_m = y_m.rearrange("p (l r) -> p r l", r=4)
                    step(dve.scalar_tensor_tensor(x_m, y_m, gate[:, bass.ds(m, 1)], x_m, ALU.mult, ALU.add))
                    dve.sem_inc(added, 1)
                step.again()



QK_BANKS = (0, 1)
V_BANK = 2
SSQ_BANKS = (3, 4)
ROT_BANKS = (5, 6)


def heads_sp(sp, M, S, w_tiles, first, tiles, turns):
    with sp.Fori(0, turns) as it:
        for j in range(tiles):
            sp.wait_ge(S.proj_done, it * tiles + (j + 1))
            sp.dma_start(M.ring[:, j], w_tiles[first + it * tiles + j]).then_inc(S.landed[j], 16)


def qkv_pe(pe, M, S, it, g, ng):
    for c in range(2):
        pe.wait_ge(S.landed[3 * g + c], it * 16 + 16)
        if c == 0:
            pe.wait_ge(S.banks_free, it * ng + (g + 1))
        for k in range(KB):
            last = pe.matmul(bank(M.ps, QK_BANKS[c]), M.ring[:, 3 * g + c, k * P:(k + 1) * P], M.h[:, k],
                             start=k == 0, stop=k == KB - 1)
        last.then_inc(S.proj_done, 1)
    pe.wait_ge(S.landed[3 * g + 2], it * 16 + 16)
    for b in range(TB):
        for k in range(KB):
            last = pe.matmul(M.ps[:, V_BANK * BANK + b * P:V_BANK * BANK + (b + 1) * P],
                             M.h[:, k, b * P:(b + 1) * P], M.ring[:, 3 * g + 2, k * P:(k + 1) * P],
                             start=k == 0, stop=k == KB - 1)
    last.then_inc(S.proj_done, 1)
    for c in range(2):
        pe.wait_ge(S.squares, it * S.per + (2 * g + c + 1))
        pe.matmul(bank(M.ps, SSQ_BANKS[c]), M.bd64[:, :], M.sq[:, c], start=True, stop=True).then_inc(S.summed, 1)
    for c in range(2):
        pe.wait_ge(S.normed, it * 2 * ng + (2 * g + c + 1))
        pe.matmul(bank(M.ps, ROT_BANKS[c]), M.rot[:, :], M.qkn[:, c], start=True, stop=True).then_inc(S.rotated, 1)


def qkv_act(act, step, M, S, it, g, ng, v_dst):
    tiles = 3 * ng
    for c in range(2):
        act.wait_ge(S.proj_done, it * tiles + (tiles + 3 * g + c + 1))
        step(act.activation(M.sq[:, c], bank(M.ps, QK_BANKS[c]), ACT.Square))
        act.sem_inc(S.squares, 1)
    act.wait_ge(S.proj_done, it * tiles + (tiles + 3 * g + 3))
    step(act.copy(v_dst, bank(M.ps, V_BANK)))
    act.sem_inc(S.v_ready, 1)
    for c in range(2):
        act.wait_ge(S.summed, it * S.per + (2 * g + c + 1))
        step(act.activation(M.ln[:, 0:T], bank(M.ps, SSQ_BANKS[c]), ACT.Ln, bias=M.eps[:, 0:1], scale=1.0 / 64))
        step(act.activation(M.rstd2[:, c], M.ln[:, 0:T], ACT.Exp, scale=-0.5))
        act.sem_inc(S.rooted, 1)


def qkv_dve(dve, step, M, S, it, g, ng, gain, q_dst, k_dst):
    for c in range(2):
        dve.wait_ge(S.rooted, it * S.per + (2 * g + c + 1))
        refine(step, dve, M.rstd2[:, c], bank(M.ps, SSQ_BANKS[c]), 1.0 / 64, M.tmp2[:, 0:T])
        step(dve.scalar_tensor_tensor(M.qkn[:, c], bank(M.ps, QK_BANKS[c]), gain[:, c:c + 1], M.rstd2[:, c],
                                      ALU.mult, ALU.mult))
        dve.sem_inc(S.normed, 1)
    for c, dst in enumerate((q_dst, k_dst)):
        step(dve.tensor_tensor(dst, M.qkn[:, c], M.cos[:, :], ALU.mult))
        dve.wait_ge(S.rotated, it * 2 * ng + (2 * g + c + 1))
        step(dve.tensor_tensor(M.tmp[:, 0:T], bank(M.ps, ROT_BANKS[c]), M.sin[:, :], ALU.mult))
        step(dve.tensor_tensor(dst, dst, M.tmp[:, 0:T], ALU.add))
    dve.sem_inc(S.qk_ready, 1)


class Named:
    pass


@contextmanager
def head_stage(nc, tiles, per):
    names = [f"landed{i}" for i in range(tiles)]
    rest = ("proj_done", "banks_free", "squares", "v_ready", "summed", "rooted", "normed", "rotated", "qk_ready",
            "scored", "peaked", "exped", "weighed", "turned", "turned_back", "valued", "stored",
            "act_done", "dve_done")
    with stage(nc, *names, *rest) as (block, *s):
        S = Named()
        S.per = per
        S.landed = s[:tiles]
        (S.proj_done, S.banks_free, S.squares, S.v_ready, S.summed, S.rooted, S.normed, S.rotated, S.qk_ready,
         S.scored, S.peaked, S.exped, S.weighed, S.turned, S.turned_back, S.valued, S.stored,
         S.act_done, S.dve_done) = s[tiles:]
        yield block, S


def diff_attention_stage(nc, M, A, w_tiles, first):
    with head_stage(nc, 3, 3) as (block, S):
        @block.sync
        def _(sp):
            heads_sp(sp, M, S, w_tiles, first, 3, HEADS_A)

        @block.tensor
        def _(pe):
            pe.sem_inc(S.proj_done, 3)
            with pe.Fori(0, HEADS_A) as h:
                qkv_pe(pe, M, S, h, 0, 1)
                pe.wait_ge(S.qk_ready, h + 1)

                def scores(b):
                    if b >= 2:
                        pe.wait_ge(S.exped, h * TB + (b - 1))
                    for c in range(2):
                        last = pe.matmul(bank(M.ps, 4 + 2 * (b % 2) + c), A.q[c * 64:(c + 1) * 64, b * P:(b + 1) * P],
                                         A.k[c * 64:(c + 1) * 64, :], start=True, stop=True)
                    last.then_inc(S.scored, 1)

                scores(0)
                scores(1)
                for b in range(TB):
                    pe.wait_ge(S.weighed, h * TB + (b + 1))
                    for n in range(TB):
                        last = pe.transpose(M.ps[:, (b % 2) * BANK + n * P:(b % 2) * BANK + (n + 1) * P],
                                            A.w[:, b % 2, n * P:(n + 1) * P], M.ident[:, :])
                    last.then_inc(S.turned, 1)
                    if b + 2 < TB:
                        scores(b + 2)
                    pe.wait_ge(S.turned_back, h * TB + (b + 1))
                    if b == 0:
                        pe.wait_ge(S.v_ready, h + 1)
                    for n in range(TB):
                        last = pe.matmul(M.ps[:, V_BANK * BANK + b * P:V_BANK * BANK + (b + 1) * P], A.v[:, n, :],
                                         A.wT[:, b % 2, n, :], start=n == 0, stop=n == TB - 1)
                    last.then_inc(S.valued, 1)
                pe.wait_ge(S.squares, h * 3 + 3)
                pe.matmul(bank(M.ps, 3), M.ones[:, :], M.sq[:, 0], start=True, stop=True).then_inc(S.summed, 1)

        @block.scalar
        def _(act):
            step = Steps(act, S.act_done)
            act.preload_act_table_set(LN_EXP)
            with act.Fori(0, HEADS_A) as h:
                qkv_act(act, step, M, S, h, 0, 1, A.v[:, :, :].rearrange("p b d -> p (b d)"))
                for b in range(TB):
                    act.wait_ge(S.peaked, h * TB + (b + 1))
                    if b >= 2:
                        act.wait_ge(S.weighed, h * TB + (b - 1))
                    for c in range(2):
                        step(act.activation(A.p[:, b % 2, c], bank(M.ps, 4 + 2 * (b % 2) + c), ACT.Exp,
                                            bias=A.peak[:, b % 2, c:c + 1], accum_out=A.z[:, b % 2, c:c + 1]))
                    act.sem_inc(S.exped, 1)
                    act.wait_ge(S.turned, h * TB + (b + 1))
                    if b >= 2:
                        act.wait_ge(S.valued, h * TB + (b - 1))
                    step(act.copy(A.wT[:, b % 2].rearrange("p n q -> p (n q)"), bank(M.ps, b % 2)))
                    act.sem_inc(S.turned_back, 1)
                act.wait_ge(S.valued, h * TB + TB)
                step(act.activation(M.sq[:, 0], bank(M.ps, V_BANK), ACT.Square))
                act.sem_inc(S.squares, 1)
                act.wait_ge(S.summed, h * 3 + 3)
                step(act.activation(M.ln[:, 0:T], bank(M.ps, 3), ACT.Ln, bias=M.eps[:, 0:1], scale=1.0 / 128))
                step(act.activation(M.rstd2[:, 0], M.ln[:, 0:T], ACT.Exp, scale=-0.5))
                act.sem_inc(S.rooted, 1)
                step.again()

        @block.vector
        def _(dve):
            step = Steps(dve, S.dve_done)
            dve.sem_inc(S.banks_free, 1)
            with dve.Fori(0, HEADS_A) as h:
                qkv_dve(dve, step, M, S, h, 0, 1, M.gain_a, A.q[:, :], A.k[:, :])

                def peak(b):
                    dve.wait_ge(S.scored, h * TB + (b + 1))
                    if b >= 2:
                        dve.wait_ge(S.exped, h * TB + (b - 1))
                    src = M.ps[:, (4 + 2 * (b % 2)) * BANK:(6 + 2 * (b % 2)) * BANK]
                    step(dve.tensor_reduce(A.peak[:, b % 2], src.rearrange("p (c k) -> p c k", c=2), X, ALU.max,
                                           negate=True))
                    dve.sem_inc(S.peaked, 1)

                peak(0)
                for b in range(TB):
                    if b + 1 < TB:
                        peak(b + 1)
                    dve.wait_ge(S.exped, h * TB + (b + 1))
                    step(dve.reciprocal(A.rz[:, :], A.z[:, b % 2]))
                    step(dve.tensor_tensor(A.rz[:, 1:2], A.rz[:, 1:2], M.nlam[:, 0:1], ALU.mult))
                    step(dve.tensor_scalar(M.tmp[:, 0:T], A.p[:, b % 2, 0], A.rz[:, 0:1], None, ALU.mult))
                    if b >= 2:
                        dve.wait_ge(S.turned, h * TB + (b - 1))
                    step(dve.scalar_tensor_tensor(A.w[:, b % 2], A.p[:, b % 2, 1], A.rz[:, 1:2], M.tmp[:, 0:T],
                                                  ALU.mult, ALU.add))
                    dve.sem_inc(S.weighed, 1)
                dve.wait_ge(S.rooted, h * 3 + 3)
                refine(step, dve, M.rstd2[:, 0], bank(M.ps, 3), 1.0 / 128, M.tmp2[:, 0:T])
                step(dve.scalar_tensor_tensor(A.oa[:, h], bank(M.ps, V_BANK), M.subln[:, 0:1], M.rstd2[:, 0],
                                              ALU.mult, ALU.mult))
                dve.sem_inc(S.banks_free, 1)
                step.again()


def window_attention_stage(nc, M, B, w_tiles, first):
    W = T + 2 * P
    with head_stage(nc, 9, 6) as (block, S):
        turns = 2 * TB

        @block.sync
        def _(sp):
            heads_sp(sp, M, S, w_tiles, first, 9, 2)

        @block.tensor
        def _(pe):
            pe.sem_inc(S.proj_done, 9)
            with pe.Fori(0, 2) as it:
                for g in range(3):
                    qkv_pe(pe, M, S, it, g, 3)
                pe.wait_ge(S.qk_ready, it * 3 + 3)

                def scores(n):
                    rows, b = slice(n // TB * 64, n // TB * 64 + 64), n % TB
                    o = (4 + 2 * (n % 2)) * BANK
                    if n >= 2:
                        pe.wait_ge(S.stored, it * turns + (n - 1))
                    pe.matmul(M.ps[:, o:o + T], B.q[rows, 0, b * P:(b + 1) * P], B.k[rows, 0, :],
                              start=True, stop=True)
                    for g in (1, 2):
                        last = pe.matmul(M.ps[:, o + T + (g - 1) * P:o + T + g * P], B.q[rows, g, b * P:(b + 1) * P],
                                         B.k[rows, g, b * P:(b + 1) * P], start=True, stop=True)
                    last.then_inc(S.scored, 1)

                scores(0)
                scores(1)
                for n in range(turns):
                    rows, b = slice(n // TB * 64, n // TB * 64 + 64), n % TB
                    pe.wait_ge(S.weighed, it * turns + (n + 1))
                    if n >= 1:
                        pe.wait_ge(S.turned_back, it * turns + n)
                    for c in range(6):
                        last = pe.transpose(M.ps[:, c * P:(c + 1) * P], B.p[:, n % 2, c * P:(c + 1) * P], M.ident[:, :])
                    last.then_inc(S.turned, 1)
                    if n + 2 < turns:
                        scores(n + 2)
                    pe.wait_ge(S.turned_back, it * turns + (n + 1))
                    if n == 0:
                        pe.wait_ge(S.v_ready, it * 3 + 3)
                    for c in range(6):
                        g, kb = (0, c) if c < TB else (c - TB + 1, b)
                        last = pe.matmul(M.ps[rows, V_BANK * BANK + b * P:V_BANK * BANK + (b + 1) * P],
                                         B.v[:, g, kb, rows], B.wT[:, n % 2, c * P:(c + 1) * P],
                                         start=c == 0, stop=c == 5)
                    last.then_inc(S.valued, 1)

        @block.scalar
        def _(act):
            step = Steps(act, S.act_done)
            act.preload_act_table_set(LN_EXP)
            with act.Fori(0, 2) as it:
                for g in range(3):
                    qkv_act(act, step, M, S, it, g, 3, B.v[:, g].rearrange("p b d -> p (b d)"))
                for n in range(turns):
                    act.wait_ge(S.peaked, it * turns + (n + 1))
                    step(act.activation(B.p[:, n % 2], B.s[:, n % 2], ACT.Exp, bias=B.peak[:, n % 2:n % 2 + 1],
                                        accum_out=B.z[:, n % 2:n % 2 + 1]))
                    act.sem_inc(S.exped, 1)
                    act.wait_ge(S.turned, it * turns + (n + 1))
                    if n >= 2:
                        act.wait_ge(S.valued, it * turns + (n - 1))
                    step(act.copy(B.wT[:, n % 2], M.ps[:, 0:W]))
                    act.sem_inc(S.turned_back, 1)
                step.again()

        @block.vector
        def _(dve):
            step = Steps(dve, S.dve_done)
            dve.sem_inc(S.banks_free, 1)
            with dve.Fori(0, 2) as it:
                for g in range(3):
                    qkv_dve(dve, step, M, S, it, g, 3, M.gain_b, B.q[:, g], B.k[:, g])
                    if g < 2:
                        dve.sem_inc(S.banks_free, 1)

                def peak(n):
                    dve.wait_ge(S.scored, it * turns + (n + 1))
                    o = (4 + 2 * (n % 2)) * BANK
                    step(dve.tensor_tensor(B.s[:, n % 2], M.ps[:, o:o + W], B.mask[:, n % TB], ALU.add))
                    dve.sem_inc(S.stored, 1)
                    step(dve.tensor_reduce(B.peak[:, n % 2:n % 2 + 1], B.s[:, n % 2], X, ALU.max, negate=True))
                    dve.sem_inc(S.peaked, 1)

                peak(0)
                for n in range(turns):
                    dve.wait_ge(S.exped, it * turns + (n + 1))
                    step(dve.reciprocal(B.rz[:, :], B.z[:, n % 2:n % 2 + 1]))
                    step(dve.tensor_scalar(B.p[:, n % 2], B.p[:, n % 2], B.rz[:, 0:1], None, ALU.mult))
                    dve.sem_inc(S.weighed, 1)
                    if n + 1 < turns:
                        peak(n + 1)
                dve.wait_ge(S.valued, it * turns + turns)
                step(dve.tensor_scalar(B.ob[:, it], bank(M.ps, V_BANK), 1.0, None, ALU.mult))
                dve.sem_inc(S.banks_free, 1)
                step.again()


def gate_stage(nc, M, A, B, w_tiles, first, wb_dram, layer):
    RING, G = 6, 2
    with stage(nc, *[f"landed{i}" for i in range(RING)], "tiles_done", "b_done", "open", "mixed",
               "act_done", "dve_done", "wb_here", "b_col") as (block, *s):
        landed, (tiles_done, b_done, opened, mixed, act_done, dve_done, wb_here, b_col) = s[:RING], s[RING:]

        @block.sync
        def _(sp):
            sp.dma_start(B.wb[:, :, :, :], wb_dram[layer]).then_inc(wb_here, 16)
            with sp.Fori(0, KB // G) as g:
                for j in range(RING):
                    sp.wait_ge(tiles_done, g * RING + (j + 1))
                    sp.dma_start(M.ring[:, j], w_tiles[first + g * RING + j]).then_inc(landed[j], 16)

        @block.tensor
        def _(pe):
            pe.sem_inc(tiles_done, RING)
            with pe.Fori(0, KB // G) as g:
                for i in range(G):
                    pe.wait_ge(mixed, g * G + (i + 1))
                    for c in range(3):
                        j = 3 * i + c
                        pe.wait_ge(landed[j], g * 16 + 16)
                        for k in range(KB):
                            rhs = A.oa[:, k] if c == 2 else M.h[:, k]
                            last = pe.matmul(bank(M.ps, 4 * i + c), M.ring[:, j, k * P:(k + 1) * P], rhs,
                                             start=k == 0, stop=k == KB - 1)
                        last.then_inc(tiles_done, 1)
                    pe.wait_ge(b_col, g * G + (i + 1))
                    for k in range(2):
                        last = pe.matmul(bank(M.ps, 4 * i + 3), B.wb2[:, i, k], B.ob[:, k], start=k == 0, stop=k == 1)
                    last.then_inc(b_done, 1)

        @block.gpsimd
        def _(pool):
            pool.wait_ge(wb_here, 16)
            with pool.Fori(0, KB // G) as g:
                for i in range(G):
                    pool.wait_ge(mixed, g * G + (i + 1))
                    pool.wait_ge(wb_here, 16)
                    pool.tensor_copy(B.wb2[:, i], B.wb[:, g * G + i]).then_inc(b_col, 1)

        @block.scalar
        def _(act):
            step = Steps(act, act_done)
            with act.Fori(0, KB // G) as g:
                for i in range(G):
                    act.wait_ge(mixed, g * G + (i + 1))
                    for c in range(2):
                        act.wait_ge(tiles_done, g * RING + (RING + 3 * i + c + 1))
                        step.hold(tiles_done)
                        step(act.activation(B.gate[:, i, c], bank(M.ps, 4 * i + c), ACT.Sigmoid,
                                            bias=M.gate_bias[:, bass.ds(g * G + (c * KB + i), 1)]))
                    act.sem_inc(opened, 1)
                step.again()

        @block.vector
        def _(dve):
            step = Steps(dve, dve_done)
            dve.sem_inc(mixed, G)
            with dve.Fori(0, KB // G) as g:
                for i in range(G):
                    dve.wait_ge(opened, g * G + (i + 1))
                    dve.wait_ge(b_done, g * G + (i + 1))
                    step(dve.tensor_tensor(M.tmp[:, 0:T], B.gate[:, i, 0], bank(M.ps, 4 * i + 2), ALU.mult))
                    step(dve.tensor_tensor(M.tmp2[:, 0:T], B.gate[:, i, 1], bank(M.ps, 4 * i + 3), ALU.mult))
                    step(dve.tensor_tensor(B.y[:, g * G + i], M.tmp[:, 0:T], M.tmp2[:, 0:T], ALU.add))
                    dve.sem_inc(mixed, 1)
                step.again()


def gated_mlp_stage(nc, M, E, u_tiles, v_tiles, first, groups, nonlinear, weights):
    G = 4
    GROUPS = groups
    SLOTS = E.slots
    weight = M.h

    with stage(nc, *[f"u_here{j}" for j in range(G)],
               "v_here", "w_here", "h_high", "h_split", "u_high", "u_ready", "v_high", "v_ready", "u_done", "activated",
               "scaled", "coef_high", "coef_ready", "v_done", "added", "act_done", "dve_done") as (block, *s):
        u_here = s[:G]
        (v_here, w_here, h_high, h_split, u_high, u_ready, v_high, v_ready, u_done, activated, scaled,
         coef_high, coef_ready, v_done, added, act_done, dve_done) = s[G:]

        @block.sync
        def _(sp):
            def load_u(g, j):
                sp.dma_start(E.raw_u[:, j], u_tiles[first * G + g * G + j]).then_inc(u_here[j], 16)

            def next_u(g, j):
                sp.wait_ge(u_ready, g * G + (j + 1))
                load_u(g + 1, j)

            for j in range(G):
                load_u(0, j)
            sp.dma_start(E.raw_v, v_tiles[first]).then_inc(v_here, 16)
            next_u(0, 0)
            next_u(0, 1)
            with sp.Fori(0, GROUPS - 2) as g:
                next_u(g, 2)
                next_u(g, 3)
                next_u(g + 1, 0)
                next_u(g + 1, 1)
                sp.wait_ge(v_ready, g * G + G)
                sp.dma_start(E.raw_v, v_tiles[first + g + 1]).then_inc(v_here, 16)
            next_u(GROUPS - 2, 2)
            next_u(GROUPS - 2, 3)
            sp.wait_ge(v_ready, (GROUPS - 1) * G)
            sp.dma_start(E.raw_v, v_tiles[first + (GROUPS - 1)]).then_inc(v_here, 16)

        if weights is not None:
            @block.gpsimd
            def _(pool):
                pool.wait_ge(h_split, KB)
                pool.dma_start(weight[:, 0:G], weights[0]).then_inc(w_here, 16)
                with pool.Fori(0, GROUPS - 1) as g:
                    pool.wait_ge(scaled, g * G + G)
                    pool.dma_start(weight[:, 0:G], weights[g + 1]).then_inc(w_here, 16)

        def ups(pe, g):
            for j in range(G):
                pe.wait_ge(u_ready, g * G + (j + 1))
                pe.wait_ge(activated, g * G + (j + 1))
                for k in range(KB):
                    for n, (a, b) in enumerate(PASSES):
                        last = pe.matmul(bank(M.ps, j), E.u[:, a, j % SLOTS, k * P:(k + 1) * P], E.h[:, b, k],
                                         start=k + n == 0, stop=k == KB - 1 and n == 2)
                last.then_inc(u_done, 1)

        def downs(pe, g):
            pe.wait_ge(v_ready, g * G + G)
            pe.wait_ge(coef_ready, g * G + 2 * G)
            for m in range(KB):
                pe.wait_ge(added, g * KB + (m + 1))
                for j in range(G):
                    for n, (a, b) in enumerate(PASSES):
                        last = pe.matmul(bank(M.ps, 4 + m % 4), E.v[:, a, j, m * P:(m + 1) * P],
                                         E.coef[:, b, j], start=j + n == 0, stop=j == G - 1 and n == 2)
                last.then_inc(v_done, 1)

        @block.tensor
        def _(pe):
            pe.sem_inc(u_done, G)
            pe.sem_inc(v_done, KB)
            pe.wait_ge(h_split, KB)
            ups(pe, 0)
            with pe.Fori(0, GROUPS - 1) as g:
                ups(pe, g + 1)
                downs(pe, g)
            downs(pe, GROUPS - 1)

        @block.scalar
        def _(act):
            step = Steps(act, act_done)
            act.sem_inc(activated, G)

            def high_u(g, j):
                act.wait_ge(u_here[j], g * 16 + 16)
                act.wait_ge(u_done, g * G + (G - SLOTS + j + 1))
                step(act.copy(E.u[:, HI, j % SLOTS], E.raw_u[:, j]))
                act.sem_inc(u_high, 1)

            def high_down(g):
                act.wait_ge(v_done, g * KB + KB)
                for j in range(G):
                    act.wait_ge(scaled, g * G + (j + 1))
                    step(act.copy(E.coef[:, HI, j], E.act[:, j]))
                    act.sem_inc(coef_high, 1)
                act.wait_ge(v_here, g * 16 + 16)
                for j in range(G):
                    step(act.copy(E.v[:, HI, j], E.raw_v[:, j]))
                    act.sem_inc(v_high, 1)

            def activations(g, more):
                for j in range(G):
                    act.wait_ge(u_done, g * G + (G + j + 1))
                    act.wait_ge(coef_ready, g * G + (j + 1))
                    step(act.activation(E.act[:, j], bank(M.ps, j), nonlinear))
                    act.sem_inc(activated, 1)
                    if j + SLOTS < G:
                        high_u(g, j + SLOTS)
                    elif more:
                        high_u(g + 1, j + SLOTS - G)

            for k in range(KB):
                step(act.copy(E.h[:, HI, k], M.h[:, k]))
                act.sem_inc(h_high, 1)
            for j in range(SLOTS):
                high_u(0, j)
            activations(0, True)
            step.again()
            with act.Fori(0, GROUPS - 2) as g:
                high_down(g)
                activations(g + 1, True)
                step.again()
            high_down(GROUPS - 2)
            activations(GROUPS - 1, False)
            high_down(GROUPS - 1)

        @block.vector
        def _(dve):
            step = Steps(dve, dve_done)
            dve.sem_inc(added, 4)
            dve.sem_inc(coef_ready, G)

            def low_u(g, j):
                dve.wait_ge(u_high, g * G + (j + 1))
                step(dve.tensor_tensor(E.u[:, LO, j % SLOTS], E.raw_u[:, j], E.u[:, HI, j % SLOTS], ALU.subtract))
                dve.sem_inc(u_ready, 1)

            def low_down(g):
                for j in range(G):
                    dve.wait_ge(coef_high, g * G + (j + 1))
                    step(dve.tensor_tensor(E.coef[:, LO, j], E.act[:, j], E.coef[:, HI, j], ALU.subtract))
                    dve.sem_inc(coef_ready, 1)
                for j in range(G):
                    dve.wait_ge(v_high, g * G + (j + 1))
                    step(dve.tensor_tensor(E.v[:, LO, j], E.raw_v[:, j], E.v[:, HI, j], ALU.subtract))
                    dve.sem_inc(v_ready, 1)

            def scales(g, more):
                if weights is not None:
                    dve.wait_ge(w_here, g * 16 + 16)
                for j in range(G):
                    dve.wait_ge(activated, g * G + (G + j + 1))
                    step(dve.tensor_tensor(E.act[:, j], E.act[:, j], E.act[:, j] if weights is None else weight[:, j], ALU.mult))
                    dve.sem_inc(scaled, 1)
                    if j + SLOTS < G:
                        low_u(g, j + SLOTS)
                    elif more:
                        low_u(g + 1, j + SLOTS - G)

            def adds(g):
                for m in range(KB):
                    dve.wait_ge(v_done, g * KB + (KB + m + 1))
                    step(dve.scalar_tensor_tensor(M.x[:, m], bank(M.ps, 4 + m % 4), M.mod[:, 5 * KB + m, 0:1], M.x[:, m],
                                                  ALU.mult, ALU.add))
                    dve.sem_inc(added, 1)

            for k in range(KB):
                dve.wait_ge(h_high, k + 1)
                step(dve.tensor_tensor(E.h[:, LO, k], M.h[:, k], E.h[:, HI, k], ALU.subtract))
                dve.sem_inc(h_split, 1)
            for j in range(SLOTS):
                low_u(0, j)
            scales(0, True)
            step.again()
            with dve.Fori(0, GROUPS - 2) as g:
                low_down(g)
                scales(g + 1, True)
                adds(g)
                step.again()
            low_down(GROUPS - 2)
            scales(GROUPS - 1, False)
            adds(GROUPS - 2)
            low_down(GROUPS - 1)
            adds(GROUPS - 1)


def setup_stage(nc, M, d):
    with stage(nc, "loaded", "act_done", "dve_done", "reduced") as (block, loaded, act_done, dve_done, reduced):
        loads = [(M.x[:, :, :], d["x"]), (M.ident[:, :], d["ident"]), (M.ones[:, :], d["ones"]),
                 (M.bd64[:, :], d["bd64"]), (M.rot[:, :], d["rot"]), (M.eps[:, :], d["eps"]),
                 (M.inv_freq[:, :], d["inv_freq"]), (M.pos[:, :], d["positions"]), (M.cond[:, :, :], d["c"]),
                 (M.g2[:, :], d["g2"])]

        @block.sync
        def _(sp):
            for dst, src in loads:
                sp.dma_start(dst, src).then_inc(loaded, 16)

        @block.vector
        def _(dve):
            step = Steps(dve, dve_done)
            dve.wait_ge(loaded, 16 * len(loads))
            MAGIC = 12582912.0
            TWO_PI = (6.28125, 0.0019350051879882812, 3.0199159819567986e-07)
            step(dve.tensor_copy(M.tmp[:, 0:T], M.pos[:, :]))
            step(dve.tensor_scalar(M.tmp[:, 0:T], M.tmp[:, 0:T], M.inv_freq[:, 0:1], None, ALU.mult))
            for dst, quarter in ((M.sin, 0.0), (M.cos, 0.25)):
                step(dve.tensor_scalar(M.tmp2[:, 0:T], M.tmp[:, 0:T], float(1 / (2 * np.pi)), quarter, ALU.mult,
                                       ALU.add))
                step(dve.tensor_scalar(M.tmp2[:, 0:T], M.tmp2[:, 0:T], MAGIC, None, ALU.add))
                step(dve.tensor_scalar(M.tmp2[:, 0:T], M.tmp2[:, 0:T], MAGIC, None, ALU.subtract))
                step(dve.scalar_tensor_tensor(dst[:, :], M.tmp2[:, 0:T], -TWO_PI[0], M.tmp[:, 0:T], ALU.mult, ALU.add))
                for part in TWO_PI[1:]:
                    step(dve.scalar_tensor_tensor(dst[:, :], M.tmp2[:, 0:T], -part, dst[:, :], ALU.mult, ALU.add))
                if quarter:
                    step(dve.tensor_scalar(dst[:, :], dst[:, :], float(np.pi / 2), None, ALU.add))
                step(dve.tensor_scalar(dst[:, :], dst[:, :], 3.1415925, -3.1415925, ALU.min, ALU.max))
            dve.sem_inc(reduced, 1)
            dve.wait_ge(act_done, 3)
            step(dve.tensor_tensor(M.cond[:, :, :], M.cond[:, :, :], M.csig[:, :, :], ALU.mult))

        @block.scalar
        def _(act):
            step = Steps(act, act_done)
            act.wait_ge(reduced, 1)
            step(act.activation(M.sin[:, :], M.sin[:, :], ACT.Sin))
            step(act.activation(M.cos[:, :], M.cos[:, :], ACT.Sin))
            step(act.activation(M.csig[:, :, :], M.cond[:, :, :], ACT.Sigmoid))


def params_stage(nc, M, A, cols_dram, wb_dram, layer):
    def col(name):
        at, n = COLS[name]
        return M.cols[:, at:at + n]

    with stage(nc, "loaded", "ready", "lam_summed", "exped", "act_done", "dve_done") as (
            block, loaded, ready, lam_summed, exped, act_done, dve_done):
        @block.sync
        def _(sp):
            sp.dma_start(M.cols[:, :], cols_dram[layer]).then_inc(loaded, 16)

        @block.vector
        def _(dve):
            step = Steps(dve, dve_done)
            dve.wait_ge(loaded, 16)
            lam = col("lam")
            step(dve.tensor_tensor(A.lam[:, 0:1], lam[:, 0:1], lam[:, 1:2], ALU.mult))
            step(dve.tensor_tensor(A.lam[:, 1:2], lam[:, 2:3], lam[:, 3:4], ALU.mult))
            dve.sem_inc(ready, 1)
            for dst, name in ((M.gain_a, "gain_a"), (M.gain_b, "gain_b")):
                step(dve.tensor_scalar(dst[:, 0:1], col(name)[:, 0:1], 0.125, None, ALU.mult))
                step(dve.tensor_copy(dst[:, 1:2], col(name)[:, 1:2]))
            step(dve.tensor_copy(M.gate_bias[:, :], col("gate_bias")))
            step(dve.tensor_tensor(M.subln[:, :], col("subln"), col("lam_init")[:, 1:2], ALU.mult))
            dve.wait_ge(exped, 1)
            step(dve.tensor_tensor(A.lam[:, 0:1], A.lam[:, 1:2], A.lam[:, 0:1], ALU.subtract))
            step(dve.tensor_tensor(M.nlam[:, :], A.lam[:, 0:1], col("lam_init")[:, 0:1], ALU.subtract))

        @block.tensor
        def _(pe):
            pe.wait_ge(ready, 1)
            pe.matmul(M.ps[:, 0:2], M.ones[:, :], A.lam[:, :], start=True, stop=True).then_inc(lam_summed, 1)

        @block.scalar
        def _(act):
            step = Steps(act, act_done)
            act.wait_ge(lam_summed, 1)
            step(act.activation(A.lam[:, :], M.ps[:, 0:2], ACT.Exp))
            act.sem_inc(exped, 1)


def mask_stage(nc, B, mask_dram):
    with stage(nc, "loaded") as (block, loaded):
        @block.sync
        def _(sp):
            sp.dma_start(B.mask[:, :, :], mask_dram).then_inc(loaded, 16)
            sp.wait_ge(loaded, 16)


def split_places(nc, ctx, name, slots):
    def split(part, *shape):
        return ctx.enter_context(nc.sbuf_tensor(f"{name}_{part}", [P, 2, *shape], F32R))

    E = Named()
    E.slots = slots
    E.h, E.u, E.v, E.coef = split("h", KB, T), split("u", slots, D), split("v", 4, D), split("coef", 4, T)
    return E


def block_one(nc, M, d):
    with ExitStack() as ctx:
        def sb(name, *shape, dt=F32):
            return ctx.enter_context(nc.sbuf_tensor(name, [P, *shape], dt))

        A, B = Named(), Named()
        A.lam = sb("lam", 2)
        def col(name):
            at, n = COLS[name]
            return M.cols[:, at:at + n]

        def mod(i):
            return M.mod[:, i * KB:(i + 1) * KB, 0]

        def x_block(k):
            return M.x[:, k]

        def h_block(k):
            return M.h[:, k]

        with nc.Fori(0, DEPTH) as layer:
            params_stage(nc, M, A, d["cols"], None, layer)
            ada_stage(nc, M, d["w_ada"], layer * 48, M.cond, 1, col("ada_b"), M.mod)
            norm_part(nc, M, x_block, T, KB, col("g_mix"), mod(1), mod(0), h_block)
            mixer = ExitStack()
            A.oa, B.ob, B.y = (mixer.enter_context(nc.sbuf_tensor(name, [P, n, T], F32))
                               for name, n in (("oa", KB), ("ob", 2), ("y", KB)))
            with ExitStack() as inner:
                def sbi(name, *shape):
                    return inner.enter_context(nc.sbuf_tensor(name, [P, *shape], F32))
                A.q, A.k = sbi("a_q", T), sbi("a_k", T)
                A.v = sbi("a_v", TB, P)
                A.p = sbi("a_p", 2, 2, T)
                A.w = sbi("a_w", 2, T)
                A.wT = sbi("a_wT", 2, TB, P)
                A.peak, A.z, A.rz = sbi("a_peak", 2, 2), sbi("a_z", 2, 2), sbi("a_rz", 2)
                diff_attention_stage(nc, M, A, d["w_a"], layer * 24)
            with ExitStack() as inner:
                def sbi(name, *shape):
                    return inner.enter_context(nc.sbuf_tensor(name, [P, *shape], F32))
                B.q, B.k = sbi("b_q", 3, T), sbi("b_k", 3, T)
                B.v = sbi("b_v", 3, TB, P)
                W = T + 2 * P
                B.s, B.p, B.wT = sbi("b_s", 2, W), sbi("b_p", 2, W), sbi("b_wT", 2, W)
                B.peak, B.z, B.rz = sbi("b_peak", 2), sbi("b_z", 2), sbi("b_rz", 1)
                B.mask = sbi("mask", TB, W)
                mask_stage(nc, B, d["mask"])
                window_attention_stage(nc, M, B, d["w_b"], layer * 18)
            with ExitStack() as inner:
                def sbi(name, *shape):
                    return inner.enter_context(nc.sbuf_tensor(name, [P, *shape], F32))
                B.gate = sbi("gate", 2, 2, T)
                B.wb, B.wb2 = sbi("wb_all", KB, 2, P), sbi("wb_two", 2, 2, P)
                gate_stage(nc, M, A, B, d["w_gate"], layer * 24, d["w_branch_b"], layer)
                residual_stage(nc, M, d["w_out"], layer * KB, B.y, mod(2), False)
            mixer.close()
            norm_part(nc, M, x_block, T, KB, col("g_mlp"), mod(4), mod(3), h_block)
            with ExitStack() as inner:
                E = split_places(nc, inner, "mlp", 2)
                E.raw_u, E.raw_v, E.act = M.ring[:, 0:4], M.ring[:, 4:8], M.scratch[:, 8:12]
                gated_mlp_stage(nc, M, E, d["w_up"], d["w_down"], layer * (FB // 4), FB // 4, ACT.Relu, None)



def cols2(M, name):
    at, n = COLS2[name]
    return M.cols2[:, at:at + n]


def conditions_stage(nc, M, d):
    with stage(nc, "loaded", "act_done", "dve_done") as (block, loaded, act_done, dve_done):
        loads = [(M.cols2[:, :], d["cols2"]), (M.ctx[:, :, :], d["ctx"]), (M.gate_row[:, :], d["gate_row"]),
                 (M.cos2[:, :], d["cos2"]), (M.sin2[:, :], d["sin2"]), (M.rot2[:, :], d["rot2"]),
                 (M.sel[:, :, :], d["sel"]), (M.decay_mask[:, :, :], d["decay_mask"]),
                 (M.starts[:, :], d["starts"])]

        @block.sync
        def _(sp):
            for dst, src in loads:
                sp.dma_start(dst, src).then_inc(loaded, 16)

        @block.scalar
        def _(act):
            step = Steps(act, act_done)
            act.wait_ge(loaded, 16 * len(loads))
            step(act.activation(M.csig2[:, :], cols2(M, "c"), ACT.Sigmoid))

        @block.vector
        def _(dve):
            step = Steps(dve, dve_done)
            dve.wait_ge(act_done, 1)
            step(dve.tensor_tensor(M.cond2[:, :, :], cols2(M, "c").rearrange("p (k c) -> p k c", c=2),
                                   M.csig2[:, :].rearrange("p (k c) -> p k c", c=2), ALU.mult))
            step(dve.tensor_scalar(M.g_qn[:, :], cols2(M, "g_qn"), float((P + 64) ** -0.5), None, ALU.mult))


def project_stage(nc, M, N, d):
    maps = [("cq", 0, True), ("cq", 1, True), ("ckv", 0, False), ("mq", 0, True), ("mq", 1, True),
            ("mk", 0, False), ("mk", 1, False), ("o", 0, True), ("o", 1, True), ("o", 2, True), ("o", 3, True)]
    with stage(nc, "whole", "tiles_here", "proj_done", "copied", "act_done") as (
            block, whole, tiles_here, proj_done, copied, act_done):
        RING = 4

        @block.sync
        def _(sp):
            sp.dma_start(N.wv[:, :, :], d["w_v2"]).then_inc(whole, 16)
            sp.dma_start(N.wkr[:, :, :], d["w_kr"]).then_inc(whole, 16)
            sp.dma_start(N.wg[:, :, :], d["w_g2"]).then_inc(whole, 16)
            for i in range(len(maps)):
                if i >= RING:
                    sp.wait_ge(proj_done, i - RING + 1)
                if i >= 1:
                    sp.wait_ge(tiles_here, 16 * i)
                sp.dma_start(M.ring[:, i % RING], d["w_in2"][i]).then_inc(tiles_here, 16)

        @block.tensor
        def _(pe):
            def pair(i):
                if i >= 4:
                    pe.wait_ge(copied, i - 3)
                return (i % 4) * 2 * BANK

            for i, (_, _, lat) in enumerate(maps):
                o = pair(i)
                pe.wait_ge(tiles_here, 16 * (i + 1))
                spans = [(CTX, T, 0)] if lat else [(0, HALF, 0), (HALF, HALF, BANK)]
                for at, n, bank_at in spans:
                    for k in range(KB):
                        last = pe.matmul(M.ps[:, o + bank_at:o + bank_at + n], M.ring[:, i % RING, k * P:(k + 1) * P],
                                         M.h[:, k, at:at + n], start=k == 0, stop=k == KB - 1)
                last.then_inc(proj_done, 1)
            pe.wait_ge(whole, 48)
            i = len(maps)
            o = pair(i)
            for half in range(2):
                for k in range(KB):
                    last = pe.matmul(M.ps[0:64, o + half * BANK:o + half * BANK + HALF], N.wkr[:, k, :],
                                     M.h[:, k, half * HALF:(half + 1) * HALF], start=k == 0, stop=k == KB - 1)
            last.then_inc(proj_done, 1)
            for b in range(AB):
                i += 1
                o = pair(i)
                for k in range(KB):
                    pe.matmul(M.ps[:, o:o + 512], M.h[:, k, b * P:(b + 1) * P], N.wv[:, k, :],
                              start=k == 0, stop=k == KB - 1)
                for k in range(KB):
                    last = pe.matmul(M.ps[:, o + BANK:o + BANK + 16], M.h[:, k, b * P:(b + 1) * P], N.wg[:, k, :],
                                     start=k == 0, stop=k == KB - 1)
                last.then_inc(proj_done, 1)

        @block.scalar
        def _(act):
            step = Steps(act, act_done)

            def two(o, rows=P):
                return M.ps[0:rows, o:o + 2 * BANK].rearrange("p (h n) -> p h n", h=2)[:, :, 0:HALF]

            for i, (name, n, lat) in enumerate(maps):
                act.wait_ge(proj_done, i + 1)
                o = (i % 4) * 2 * BANK
                if name == "cq":
                    step(act.copy(N.cq[:, n], M.ps[:, o:o + T]))
                elif name == "ckv":
                    step(act.copy(N.ckv[:, :].rearrange("p (h n) -> p h n", h=2), two(o)))
                elif name == "mq":
                    step(act.copy(N.mq_raw[:, n, 1:1 + T], M.ps[:, o:o + T]))
                elif name == "mk":
                    step(act.copy(N.mk_raw[:, n, 1:1 + CTX], M.ps[:, o:o + CTX]))
                    step(act.copy(N.mk_raw[:, n, CTX + 3:HALF + 3], M.ps[:, o + CTX:o + HALF]))
                    step(act.copy(N.mk_raw[:, n, HALF + 3:TA + 3], M.ps[:, o + BANK:o + BANK + HALF]))
                else:
                    step(act.activation(N.o[:, n], M.ps[:, o:o + T], ACT.Sigmoid))
                act.sem_inc(copied, 1)
            i = len(maps)
            act.wait_ge(proj_done, i + 1)
            step(act.copy(N.kr[0:64, :].rearrange("p (h n) -> p h n", h=2), two((i % 4) * 2 * BANK, 64)))
            act.sem_inc(copied, 1)
            for b in range(AB):
                i += 1
                o = (i % 4) * 2 * BANK
                act.wait_ge(proj_done, i + 1)
                step(act.copy(N.v[:, b], M.ps[:, o:o + 512]))
                step(act.copy(N.gates[:, b], M.ps[:, o + BANK:o + BANK + 16]))
                act.sem_inc(copied, 1)


def latent_norm_stage(nc, M, N):
    with stage(nc, "squares", "summed", "rooted", "act_done", "dve_done") as (
            block, squares, summed, rooted, act_done, dve_done):
        @block.scalar
        def _(act):
            step = Steps(act, act_done)
            act.preload_act_table_set(LN_EXP)
            step(act.activation(M.sq[:, :, :], N.cq[:, :, :], ACT.Square))
            step(act.activation(N.sqk[:, :], N.ckv[:, :], ACT.Square))
            act.sem_inc(squares, 1)
            act.wait_ge(summed, 1)
            step(act.activation(M.ln[:, 0:T], bank(M.ps, 0), ACT.Ln, bias=M.eps[:, 0:1], scale=1.0 / 256))
            step(act.activation(M.rstd[:, 0:T], M.ln[:, 0:T], ACT.Exp, scale=-0.5))
            step(act.activation(N.lnk[:, :].rearrange("p (h n) -> p h n", h=2),
                                M.ps[:, 2 * BANK:4 * BANK].rearrange("p (h n) -> p h n", h=2)[:, :, 0:HALF],
                                ACT.Ln, bias=M.eps[:, 0:1], scale=1.0 / 128))
            step(act.activation(N.rk[:, :], N.lnk[:, :], ACT.Exp, scale=-0.5))
            act.sem_inc(rooted, 1)

        @block.tensor
        def _(pe):
            pe.wait_ge(squares, 1)
            for n in range(2):
                pe.matmul(bank(M.ps, 0), M.ones[:, :], M.sq[:, n], start=n == 0, stop=n == 1)
            for half in range(2):
                last = pe.matmul(bank(M.ps, 2 + half, HALF), M.ones[:, :], N.sqk[:, half * HALF:(half + 1) * HALF],
                                 start=True, stop=True)
            last.then_inc(summed, 1)

        @block.vector
        def _(dve):
            step = Steps(dve, dve_done)
            dve.wait_ge(rooted, 1)
            refine(step, dve, M.rstd[:, 0:T], bank(M.ps, 0), 1.0 / 256, M.tmp2[:, 0:T])
            refine(step, dve, N.rk[:, :].rearrange("p (h n) -> p h n", h=2),
                   M.ps[:, 2 * BANK:4 * BANK].rearrange("p (h n) -> p h n", h=2)[:, :, 0:HALF], 1.0 / 128,
                   N.work[:, :].rearrange("p (h n) -> p h n", h=2))
            for n in range(2):
                step(dve.scalar_tensor_tensor(N.cq[:, n], N.cq[:, n], cols2(M, "g_cq")[:, n:n + 1], M.rstd[:, 0:T],
                                              ALU.mult, ALU.mult))
            step(dve.scalar_tensor_tensor(N.ckv[:, :], N.ckv[:, :], cols2(M, "g_ckv"), N.rk[:, :],
                                          ALU.mult, ALU.mult))


def mla_stage(nc, M, N, R, d):
    def halves(i, rows=P):
        return M.ps[0:rows, i * BANK:(i + 2) * BANK].rearrange("p (h n) -> p h n", h=2)[:, :, 0:HALF]

    def split(ap):
        return ap.rearrange("p (h n) -> p h n", h=2)

    with stage(nc, "w_here", "w_used", "q_done", "k_done", "v_done", "q_squares", "k_squares", "q_summed", "k_summed",
               "q_root", "k_root", "v_ready", "normed", "rotated", "qk_ready", "scored", "peaked", "exped", "weighed",
               "turned", "turned_back", "valued", "taken", "act_done", "dve_done") as (
            block, w_here, w_used, q_done, k_done, v_done, q_squares, k_squares, q_summed, k_summed,
            q_root, k_root, v_ready, normed, rotated, qk_ready, scored, peaked, exped, weighed,
            turned, turned_back, valued, taken, act_done, dve_done):

        @block.sync
        def _(sp):
            with sp.Fori(0, MLA_HEADS) as h:
                sp.wait_ge(w_used, h + 1)
                sp.dma_start(R.w[:, :], d["w_mla"][h]).then_inc(w_here, 16)

        @block.tensor
        def _(pe):
            pe.sem_inc(w_used, 1)
            with pe.Fori(0, MLA_HEADS) as h:
                pe.wait_ge(w_here, h * 16 + 16)
                pe.wait_ge(taken, h + 1)
                for k in range(2):
                    pe.matmul(bank(M.ps, 0), R.w[:, k * 192:k * 192 + P], N.cq[:, k], start=k == 0, stop=k == 1)
                for k in range(2):
                    last = pe.matmul(M.ps[0:64, BANK:2 * BANK], R.w[:, k * 192 + P:(k + 1) * 192], N.cq[:, k],
                                     start=k == 0, stop=k == 1)
                last.then_inc(q_done, 1)
                for half in range(2):
                    last = pe.matmul(bank(M.ps, 2 + half, HALF), R.w[:, 384:512],
                                     N.ckv[:, half * HALF:(half + 1) * HALF], start=True, stop=True)
                last.then_inc(k_done, 1)
                for b in range(AB):
                    last = pe.matmul(M.ps[:, 4 * BANK + b * P:4 * BANK + (b + 1) * P], N.ckv[:, b * P:(b + 1) * P],
                                     R.w[:, 512:640], start=True, stop=True)
                last.then_inc(v_done, 1)
                pe.wait_ge(q_squares, h + 1)
                pe.matmul(bank(M.ps, 6), M.ones[:, :], M.sq[:, 0], start=True, stop=False)
                pe.matmul(bank(M.ps, 6), M.ones[0:64, :], M.sq[0:64, 1], start=False, stop=True).then_inc(q_summed, 1)
                pe.wait_ge(k_squares, h + 1)
                pe.wait_ge(normed, h * 2 + 1)
                for half in range(2):
                    pe.matmul(bank(M.ps, 6 + half, HALF), M.ones[:, :], R.sq[:, half * HALF:(half + 1) * HALF],
                              start=True, stop=False)
                    last = pe.matmul(bank(M.ps, 6 + half, HALF), M.ones[0:64, :],
                                     R.sqr[0:64, half * HALF:(half + 1) * HALF], start=False, stop=True)
                last.then_inc(k_summed, 1)
                pe.wait_ge(normed, h * 2 + 1)
                pe.matmul(M.ps[:, BANK:2 * BANK], M.rot2[0:64, :], R.qr[0:64, :], start=True,
                          stop=True).then_inc(rotated, 1)
                pe.wait_ge(normed, h * 2 + 2)
                for half in range(2):
                    last = pe.matmul(M.ps[:, (2 + half) * BANK:(2 + half) * BANK + HALF], M.rot2[0:64, :],
                                     R.kr[0:64, half * HALF:(half + 1) * HALF], start=True, stop=True)
                last.then_inc(rotated, 1)
                pe.wait_ge(qk_ready, h + 1)
                pe.wait_ge(v_ready, h + 1)

                def scores(b):
                    if b >= 2:
                        pe.wait_ge(exped, h * TB + (b - 1))
                    for half in range(2):
                        o = (4 + 2 * (b % 2) + half) * BANK
                        pe.matmul(M.ps[:, o:o + HALF], R.qn[:, b * P:(b + 1) * P],
                                  R.kn[:, half * HALF:(half + 1) * HALF], start=True, stop=False)
                        last = pe.matmul(M.ps[:, o:o + HALF], R.qr[0:64, b * P:(b + 1) * P],
                                         R.kr[0:64, half * HALF:(half + 1) * HALF], start=False, stop=True)
                    last.then_inc(scored, 1)

                scores(0)
                scores(1)
                for b in range(TB):
                    pe.wait_ge(weighed, h * TB + (b + 1))
                    if b >= 1:
                        pe.wait_ge(turned_back, h * TB + b)
                    for c in range(AB):
                        last = pe.transpose(M.ps[:, c * P:(c + 1) * P], R.p[:, b % 2, c * P:(c + 1) * P], M.ident[:, :])
                    last.then_inc(turned, 1)
                    if b + 2 < TB:
                        scores(b + 2)
                    pe.wait_ge(turned_back, h * TB + (b + 1))
                    for c in range(AB):
                        last = pe.matmul(M.ps[:, 2 * BANK + b * P:2 * BANK + (b + 1) * P], R.v[:, c, :],
                                         R.pT[:, b % 2, c * P:(c + 1) * P], start=c == 0, stop=c == AB - 1)
                    last.then_inc(valued, 1)
                pe.sem_inc(w_used, 1)

        @block.scalar
        def _(act):
            step = Steps(act, act_done)
            act.preload_act_table_set(LN_EXP)
            with act.Fori(0, MLA_HEADS) as h:
                act.wait_ge(q_done, h + 1)
                step(act.activation(M.sq[:, 0], bank(M.ps, 0), ACT.Square))
                step(act.activation(M.sq[0:64, 1], M.ps[0:64, BANK:2 * BANK], ACT.Square))
                act.sem_inc(q_squares, 1)
                act.wait_ge(k_done, h + 1)
                step(act.activation(split(R.sq[:, :]), halves(2), ACT.Square))
                step(act.activation(R.sqr[0:64, :], N.kr[0:64, :], ACT.Square))
                act.sem_inc(k_squares, 1)
                act.wait_ge(v_done, h + 1)
                step(act.copy(R.v[:, :, :].rearrange("p b d -> p (b d)"), M.ps[:, 4 * BANK:4 * BANK + TA]))
                act.sem_inc(v_ready, 1)
                act.wait_ge(q_summed, h + 1)
                step(act.activation(M.ln[:, 0:T], bank(M.ps, 6), ACT.Ln, bias=M.eps[:, 0:1], scale=1.0 / 192))
                step(act.activation(M.rstd[:, 0:T], M.ln[:, 0:T], ACT.Exp, scale=-0.5))
                act.sem_inc(q_root, 1)
                act.wait_ge(k_summed, h + 1)
                step(act.activation(split(N.lnk[:, :]), halves(6), ACT.Ln, bias=M.eps[:, 0:1], scale=1.0 / 192))
                step(act.activation(N.rk[:, :], N.lnk[:, :], ACT.Exp, scale=-0.5))
                act.sem_inc(k_root, 1)
                for b in range(TB):
                    act.wait_ge(peaked, h * TB + (b + 1))
                    if b >= 2:
                        act.wait_ge(turned, h * TB + (b - 1))
                    step(act.activation(split(R.p[:, b % 2]), halves(4 + 2 * (b % 2)), ACT.Exp,
                                        bias=R.peak[:, b % 2:b % 2 + 1], accum_out=R.z[:, b % 2:b % 2 + 1]))
                    act.sem_inc(exped, 1)
                    act.wait_ge(turned, h * TB + (b + 1))
                    if b >= 2:
                        act.wait_ge(valued, h * TB + (b - 1))
                    step(act.copy(R.pT[:, b % 2], M.ps[:, 0:TA]))
                    act.sem_inc(turned_back, 1)
                step.again()

        @block.vector
        def _(dve):
            step = Steps(dve, dve_done)
            dve.sem_inc(taken, 1)
            with dve.Fori(0, MLA_HEADS) as h:
                g_qn, g_kn = M.g_qn, cols2(M, "g_kn")
                dve.wait_ge(q_root, h + 1)
                refine(step, dve, M.rstd[:, 0:T], bank(M.ps, 6), 1.0 / 192, M.tmp2[:, 0:T])
                step(dve.scalar_tensor_tensor(R.qn[:, :], bank(M.ps, 0), g_qn[:, 0:1], M.rstd[:, 0:T],
                                              ALU.mult, ALU.mult))
                step(dve.scalar_tensor_tensor(R.qr[0:64, :], M.ps[0:64, BANK:2 * BANK], g_qn[0:64, 1:2],
                                              M.rstd[0:64, 0:T], ALU.mult, ALU.mult))
                dve.sem_inc(normed, 1)
                dve.wait_ge(k_root, h + 1)
                refine(step, dve, split(N.rk[:, :]), halves(6), 1.0 / 192, split(R.tmp[:, :]))
                step(dve.scalar_tensor_tensor(split(R.kn[:, :]), halves(2), g_kn[:, 0:1], split(N.rk[:, :]),
                                              ALU.mult, ALU.mult))
                step(dve.scalar_tensor_tensor(R.kr[0:64, :], N.kr[0:64, :], g_kn[0:64, 1:2], N.rk[0:64, :],
                                              ALU.mult, ALU.mult))
                dve.sem_inc(normed, 1)
                dve.wait_ge(rotated, h * 2 + 1)
                step(dve.tensor_tensor(M.tmp[0:64, 0:T], M.ps[0:64, BANK:2 * BANK], M.sin2[0:64, CTX:TA], ALU.mult))
                step(dve.tensor_tensor(R.qr[0:64, :], R.qr[0:64, :], M.cos2[0:64, CTX:TA], ALU.mult))
                step(dve.tensor_tensor(R.qr[0:64, :], R.qr[0:64, :], M.tmp[0:64, 0:T], ALU.add))
                dve.wait_ge(rotated, h * 2 + 2)
                step(dve.tensor_tensor(split(R.tmp[0:64, :]), halves(2, 64), split(M.sin2[0:64, :]), ALU.mult))
                step(dve.tensor_tensor(R.kr[0:64, :], R.kr[0:64, :], M.cos2[0:64, :], ALU.mult))
                step(dve.tensor_tensor(R.kr[0:64, :], R.kr[0:64, :], R.tmp[0:64, :], ALU.add))
                dve.sem_inc(qk_ready, 1)

                def peak(b):
                    dve.wait_ge(scored, h * TB + (b + 1))
                    if b >= 2:
                        dve.wait_ge(exped, h * TB + (b - 1))
                    step(dve.tensor_reduce(R.peak[:, b % 2:b % 2 + 1], halves(4 + 2 * (b % 2)),
                                           mybir.AxisListType.XY, ALU.max, negate=True))
                    dve.sem_inc(peaked, 1)

                peak(0)
                for b in range(TB):
                    if b + 1 < TB:
                        peak(b + 1)
                    dve.wait_ge(exped, h * TB + (b + 1))
                    step(dve.reciprocal(R.rz[:, :], R.z[:, b % 2:b % 2 + 1]))
                    step(dve.tensor_scalar(R.p[:, b % 2], R.p[:, b % 2], R.rz[:, 0:1], None, ALU.mult))
                    dve.sem_inc(weighed, 1)
                dve.wait_ge(valued, h * TB + TB)
                step(dve.tensor_scalar(N.mix[:, h], bank(M.ps, 2), 1.0, None, ALU.mult))
                dve.sem_inc(taken, 1)
                step.again()


def conv_stage(nc, M, N):
    with stage(nc, "bordered", "convolved", "opened", "biased", "logs", "forget_ready", "rowed", "act_done",
               "dve_done", "pool_done") as (
            block, bordered, convolved, opened, biased, logs, forget_ready, rowed, act_done, dve_done, pool_done):
        conv = cols2(M, "conv")
        jobs = [(N.mq_raw[:, n], n, T, 0, N.mq[:, n], 0, 0.125) for n in range(2)]
        jobs += [(N.mk_raw[:, n], 2 + n, CTX, 0, N.mk[:, n], 0, 1.0) for n in range(2)]
        jobs += [(N.mk_raw[:, n], 2 + n, T, CTX + 2, N.mk[:, n], CTX, 1.0) for n in range(2)]

        @block.gpsimd
        def _(pool):
            step = Steps(pool, pool_done)
            for raw, at in ((N.mq_raw, 0), (N.mq_raw, T + 1), (N.mk_raw, 0), (N.mk_raw, CTX + 1),
                            (N.mk_raw, CTX + 2), (N.mk_raw, TA + 3)):
                step(pool.memset(raw[:, :, at:at + 1], 0.0))
            pool.sem_inc(bordered, 1)

        @block.vector
        def _(dve):
            step = Steps(dve, dve_done)
            for b in range(AB):
                step(dve.tensor_tensor(N.gates[:, b], N.gates[:, b], M.gate_row[:, :], ALU.add))
            f = N.gates[:, :, 8:16]
            step(dve.scalar_tensor_tensor(N.fabs[:, :, :], f, -1.0, f, ALU.mult, ALU.min))
            dve.sem_inc(biased, 1)
            dve.wait_ge(logs, 1)
            step(dve.scalar_tensor_tensor(f, f, 0.0, N.fabs[:, :, :], ALU.min, ALU.subtract))
            dve.sem_inc(forget_ready, 1)
            dve.wait_ge(bordered, 1)
            for j, (raw, ch, n, at, dst, to, scale) in enumerate(jobs):
                y = N.conv[:, j % 2, 0:n]
                step(dve.tensor_scalar(y, raw[:, at + 1:at + 1 + n], conv[:, 4 + ch:5 + ch], None, ALU.mult))
                step(dve.scalar_tensor_tensor(y, raw[:, at:at + n], conv[:, ch:ch + 1], y, ALU.mult, ALU.add))
                step(dve.scalar_tensor_tensor(y, raw[:, at + 2:at + 2 + n], conv[:, 8 + ch:9 + ch], y,
                                              ALU.mult, ALU.add))
                dve.sem_inc(convolved, 1)
                dve.wait_ge(opened, j + 1)
                step(dve.scalar_tensor_tensor(dst[:, to:to + n], y, scale, N.conv_sig[:, j % 2, 0:n],
                                              ALU.mult, ALU.mult))
            dve.wait_ge(rowed, 1)
            step(dve.memset(N.rows[:, :, :], 0.0))
            for kind in range(2):
                src = M.ps[:, kind * 2 * BANK:kind * 2 * BANK + TA]
                step(dve.tensor_copy(N.rows[0:4, kind, :], src[0:4, :]))
                for lo, hi in ((0, CTX), (CTX, TA)):
                    step(dve.tensor_copy(N.rows[32:36, kind, lo:hi], src[32:36, lo:hi][:, ::-1]))

        @block.scalar
        def _(act):
            step = Steps(act, act_done)
            act.wait_ge(biased, 1)
            step(act.activation(N.fabs[:, :, :], N.fabs[:, :, :], ACT.Exp))
            step(act.activation(N.fabs[:, :, :], N.fabs[:, :, :], ACT.Ln, bias=1.0))
            act.sem_inc(logs, 1)
            for j, (raw, ch, n, at, dst, to, scale) in enumerate(jobs):
                act.wait_ge(convolved, j + 1)
                step(act.activation(N.conv_sig[:, j % 2, 0:n], N.conv[:, j % 2, 0:n], ACT.Sigmoid))
                act.sem_inc(opened, 1)

        @block.tensor
        def _(pe):
            pe.wait_ge(forget_ready, 1)
            for kind in range(2):
                for way in range(2):
                    for b in range(AB):
                        at = kind * 8 + way * 4
                        o = kind * 2 * BANK + b * P
                        last = pe.matmul(M.ps[way * 32:way * 32 + 4, o:o + P], N.gates[:, b, at:at + 4],
                                         M.ident[:, :], start=True, stop=True)
            last.then_inc(rowed, 1)


def decay_stage(nc, M, N, Z):
    I_, LF, MT, F_, A_, D_ = range(6)
    with stage(nc, "rows_ready", "spread", "spread_taken", "act_done", "dve_done") as (
            block, rows_ready, spread, spread_taken, act_done, dve_done):
        R36 = 36

        @block.vector
        def _(dve):
            step = Steps(dve, dve_done)
            r = N.rows
            step(dve.tensor_tensor_scan(r[0:R36, MT, :], r[0:R36, LF, :], r[0:R36, I_, :], 0.0, ALU.add, ALU.max))
            step(dve.tensor_tensor_scan(r[0:R36, F_, :], M.starts[0:R36, :], r[0:R36, LF, :], 0.0,
                                        ALU.mult, ALU.add))
            step(dve.tensor_tensor(r[0:R36, A_, :], r[0:R36, F_, :], r[0:R36, MT, :], ALU.subtract))
            step(dve.tensor_tensor(r[0:R36, D_, :], r[0:R36, I_, :], r[0:R36, F_, :], ALU.subtract))
            for kind in (MT, F_, A_, D_):
                step(dve.tensor_copy(N.nat[0:R36, kind, :], r[0:R36, kind, :]))
                for lo, hi in ((0, CTX), (CTX, TA)):
                    step(dve.tensor_copy(N.nat[32:36, kind, lo:hi], r[32:36, kind, lo:hi][:, ::-1]))
            for way in range(2):
                rows = slice(way * 32, way * 32 + 4)
                last = P - 1 if way == 0 else 0
                step(dve.tensor_copy(N.tot[rows, :],
                                     N.nat[rows, F_, :].rearrange("p (b t) -> p b t", b=AB)[:, :, last]))
            dve.sem_inc(rows_ready, 1)
            dve.wait_ge(spread, 1)
            for way in range(2):
                step(dve.tensor_copy(N.dcol[:, way], bank(M.ps, 2 * way, 24).rearrange("p (b h) -> p b h", b=AB)))
                step(dve.tensor_copy(N.totb[:, way * 4:way * 4 + 4],
                                     bank(M.ps, 2 * way + 1, 24).rearrange("p (c b) -> p c b", c=4)))
            for way in range(2):
                order = [0, 1, 2, 3, 4, 5] if way == 0 else [1, 0, 5, 4, 3, 2]
                for h in range(4):
                    c = way * 4 + h
                    for n, a in enumerate(order):
                        if n:
                            was = order[n - 1]
                            for b in order[:n]:
                                step(dve.tensor_tensor(Z.bias[:, c, a, b:b + 1], Z.bias[:, c, was, b:b + 1],
                                                       N.totb[:, c, was:was + 1], ALU.add))
                        step(dve.tensor_copy(Z.bias[:, c, a, a:a + 1], N.dcol[:, way, a, h:h + 1]))

        @block.tensor
        def _(pe):
            pe.wait_ge(rows_ready, 1)
            for way in range(2):
                rows = slice(way * 32, way * 32 + 4)
                for b in range(AB):
                    o = way * 2 * BANK + b * 4
                    pe.matmul(M.ps[:, o:o + 4], N.nat[rows, D_, b * P:(b + 1) * P], M.ident[rows, rows],
                              start=True, stop=True)
            for c in range(8):
                rows = slice(c // 4 * 32, c // 4 * 32 + 4)
                o = (c // 4 * 2 + 1) * BANK + c % 4 * AB
                last = pe.matmul(M.ps[:, o:o + AB], M.sel[rows, c, :], N.tot[rows, :],
                                 start=True, stop=True)
            last.then_inc(spread, 1)


def mlstm_stage(nc, M, N, Z):
    MT, A_ = 2, 4
    combos = [(way, h) for h in range(4) for way in range(2)]

    def span(way, b):
        if b < 2:
            return 0, T
        return ((b - 2) * P, T) if way == 0 else (0, (b - 1) * P)

    with stage(nc, "spread", "masked", "scored", "decayed", "weighed", "summed", "a_used", "h_done", "em_ready",
               "act_done", "dve_done") as (
            block, spread, masked, scored, decayed, weighed, summed, a_used, h_done, em_ready, act_done, dve_done):
        @block.tensor
        def _(pe):
            n = 0
            for c, (way, h) in enumerate(combos):
                rows = slice(way * 32, way * 32 + 4)
                if c:
                    pe.wait_ge(a_used, c)
                pe.matmul(bank(M.ps, 0), M.sel[rows, way * 4 + h, :], N.nat[rows, A_, CTX:TA], start=True, stop=True)
                pe.matmul(bank(M.ps, 1), M.sel[rows, way * 4 + h, :], N.nat[rows, MT, CTX:TA], start=True,
                          stop=True).then_inc(spread, 1)
                f = slice(h % 2 * 64, h % 2 * 64 + 64)

                def scores(b, at):
                    lo, hi = span(way, b)
                    if at >= 2:
                        pe.wait_ge(weighed, at - 1)
                    pe.matmul(M.ps[:, (2 + at % 2) * BANK + lo:(2 + at % 2) * BANK + hi],
                              N.mk[f, h // 2, b * P:(b + 1) * P], N.mq[f, h // 2, lo:hi], start=True,
                              stop=True).then_inc(scored, 1)

                scores(0, n)
                for b in range(AB):
                    if b + 1 < AB:
                        scores(b + 1, n + b + 1)
                    lo, hi = span(way, b)
                    pe.wait_ge(weighed, n + b + 1)
                    if b == 0 and c:
                        pe.wait_ge(h_done, c)
                    pe.matmul(M.ps[:, 4 * BANK + lo:4 * BANK + hi], N.v[:, b, h * P:(h + 1) * P],
                              Z.w[:, (n + b) % 2, lo:hi], start=b == 0, stop=b == AB - 1)
                    pe.matmul(M.ps[:, 5 * BANK + lo:5 * BANK + hi], M.ones[:, :], Z.w[:, (n + b) % 2, lo:hi],
                              start=b == 0, stop=b == AB - 1).then_inc(summed, 1)
                n += AB

        @block.scalar
        def _(act):
            step = Steps(act, act_done)
            n = 0
            for c, (way, h) in enumerate(combos):
                act.wait_ge(masked, c + 1)
                step(act.activation(Z.em[:, :], bank(M.ps, 1), ACT.Exp, scale=-1.0))
                act.sem_inc(em_ready, 1)
                for b in range(AB):
                    lo, hi = span(way, b)
                    if n + b >= 2:
                        act.wait_ge(weighed, n + b - 1)
                    for a in range(lo // P, hi // P):
                        diagonal = b == a + 2
                        src = Z.am if diagonal else Z.a
                        step(act.activation(Z.e[:, (n + b) % 2, a * P:(a + 1) * P], src[:, a * P:(a + 1) * P], ACT.Exp,
                                            bias=Z.bias[:, way * 4 + h, a + 2, b:b + 1]))
                    act.sem_inc(decayed, 1)
                n += AB

        @block.vector
        def _(dve):
            step = Steps(dve, dve_done)
            n = 0
            for c, (way, h) in enumerate(combos):
                dve.wait_ge(spread, c + 1)
                step(dve.tensor_copy(Z.a[:, :], bank(M.ps, 0)))
                step(dve.tensor_tensor(Z.am[:, :], bank(M.ps, 0), M.decay_mask[:, way, :], ALU.add))
                dve.sem_inc(masked, 1)
                for b in range(AB):
                    lo, hi = span(way, b)
                    dve.wait_ge(decayed, n + b + 1)
                    dve.wait_ge(scored, n + b + 1)
                    if n + b >= 2:
                        dve.wait_ge(summed, n + b - 1)
                    o = (2 + (n + b) % 2) * BANK
                    step(dve.tensor_tensor(Z.w[:, (n + b) % 2, lo:hi], Z.e[:, (n + b) % 2, lo:hi],
                                           M.ps[:, o + lo:o + hi], ALU.mult))
                    dve.sem_inc(weighed, 1)
                dve.wait_ge(em_ready, c + 1)
                dve.sem_inc(a_used, 1)
                dve.wait_ge(summed, n + AB)
                step(dve.scalar_tensor_tensor(Z.den[:, :], bank(M.ps, 5), -1.0, Z.em[:, :], ALU.mult, ALU.max))
                step(dve.tensor_tensor(Z.den[:, :], bank(M.ps, 5), Z.den[:, :], ALU.max))
                step(dve.reciprocal(Z.den[:, :], Z.den[:, :]))
                if way == 0:
                    step(dve.tensor_tensor(Z.hs[:, h], bank(M.ps, 4), Z.den[:, :], ALU.mult))
                else:
                    step(dve.tensor_tensor(Z.den[:, :], bank(M.ps, 4), Z.den[:, :], ALU.mult))
                    step(dve.tensor_tensor(Z.hs[:, h], Z.hs[:, h], Z.den[:, :], ALU.add))
                dve.sem_inc(h_done, 1)
                n += AB


def mlstm_out_stage(nc, M, N, Z):
    with stage(nc, "squares", "summed", "rooted", "act_done", "dve_done") as (
            block, squares, summed, rooted, act_done, dve_done):
        @block.scalar
        def _(act):
            step = Steps(act, act_done)
            act.preload_act_table_set(LN_EXP)
            for h in range(4):
                if h >= 2:
                    act.wait_ge(summed, h - 1)
                step(act.activation(M.sq[:, h % 2], Z.hs[:, h], ACT.Square))
                act.sem_inc(squares, 1)
            for h in range(4):
                act.wait_ge(summed, h + 1)
                step(act.activation(Z.lns[:, h], bank(M.ps, h), ACT.Ln, bias=M.eps[:, 0:1], scale=1.0 / 128))
            step(act.activation(Z.lns[:, :, :], Z.lns[:, :, :], ACT.Exp, scale=-0.5))
            act.sem_inc(rooted, 1)

        @block.tensor
        def _(pe):
            for h in range(4):
                pe.wait_ge(squares, h + 1)
                pe.matmul(bank(M.ps, h), M.ones[:, :], M.sq[:, h % 2], start=True, stop=True).then_inc(summed, 1)

        @block.vector
        def _(dve):
            step = Steps(dve, dve_done)
            dve.wait_ge(rooted, 1)
            for h in range(4):
                refine(step, dve, Z.lns[:, h], bank(M.ps, h), 1.0 / 128, M.tmp2[:, 0:T])
                step(dve.scalar_tensor_tensor(Z.hs[:, h], Z.hs[:, h], cols2(M, "g_ml")[:, h:h + 1], Z.lns[:, h],
                                              ALU.mult, ALU.mult))
                step(dve.tensor_tensor(N.mix[:, 4 + h], Z.hs[:, h], N.o[:, h], ALU.mult))



def query_stage(nc, M, Q, w_tiles, sub_keys):
    HP = 2 * PEER_HEADS
    G = 2
    with stage(nc, *[f"landed{i}" for i in range(G)], *[f"keys{i}" for i in range(G)], "q_done", "q_copied", "scored",
               "s_copied", "act_done", "dve_done") as (block, *s):
        landed, keys, (q_done, q_copied, scored, s_copied, act_done, dve_done) = s[:G], s[G:2 * G], s[2 * G:]

        @block.sync
        def _(sp):
            with sp.Fori(0, HP // G) as g:
                for j in range(G):
                    sp.wait_ge(scored, g * G + (j + 1))
                    sp.dma_start(M.ring[:, j], w_tiles[g * G + j]).then_inc(landed[j], 16)
                    sp.dma_start(Q.keys[:, j], sub_keys[g * G + j]).then_inc(keys[j], 16)

        @block.tensor
        def _(pe):
            pe.sem_inc(scored, G)
            with pe.Fori(0, HP // G) as g:
                for j in range(G):
                    pe.wait_ge(landed[j], g * 16 + 16)
                    pe.wait_ge(q_copied, g * G + (j + 1))
                    for k in range(KB):
                        last = pe.matmul(bank(M.ps, j), M.ring[:, j, k * P:(k + 1) * P], M.h[:, k],
                                         start=k == 0, stop=k == KB - 1)
                    last.then_inc(q_done, 1)
                    pe.wait_ge(keys[j], g * 16 + 16)
                    pe.wait_ge(q_copied, g * G + (G + j + 1))
                    pe.wait_ge(s_copied, g * G + (j + 1))
                    for b in range(TB):
                        last = pe.matmul(M.ps[:, (2 + j) * BANK + b * P:(2 + j) * BANK + (b + 1) * P],
                                         Q.q[:, j, b * P:(b + 1) * P], Q.keys[:, j], start=True, stop=True)
                    last.then_inc(scored, 1)

        @block.scalar
        def _(act):
            step = Steps(act, act_done)
            act.sem_inc(q_copied, G)
            with act.Fori(0, HP // G) as g:
                for j in range(G):
                    act.wait_ge(q_done, g * G + (j + 1))
                    step(act.copy(Q.q[:, j], bank(M.ps, j)))
                    act.sem_inc(q_copied, 1)
                step.again()

        @block.vector
        def _(dve):
            step = Steps(dve, dve_done)
            dve.sem_inc(s_copied, G)
            with dve.Fori(0, HP // G) as g:
                for j in range(G):
                    dve.wait_ge(scored, g * G + (G + j + 1))
                    step(dve.tensor_copy(Q.s[:, j].rearrange("p b k -> p (b k)"), bank(M.ps, 2 + j)))
                    dve.sem_inc(s_copied, 1)
                    for b in range(TB):
                        top_sixteen(dve, step, Q.s[:, j, b], Q.top[:, b], Q.at[:, b])
                    step(dve.tensor_scalar(Q.sv[:, :, g * G + j], Q.top[:, :, :], 1.0, None, ALU.mult))
                    step(dve.tensor_scalar(Q.si[:, :, g * G + j], Q.at[:, :, :], 1.0, None, ALU.mult))
                step.again()


def top_sixteen(dve, step, values, top, at):
    step(dve.max(top[:, 0:8], values))
    step(dve.max_index(at[:, 0:8], top[:, 0:8], values))
    step(dve.match_replace(values, top[:, 0:8], values, -3.0e38))
    step(dve.max(top[:, 8:16], values))
    step(dve.max_index(at[:, 8:16], top[:, 8:16], values))


def choice_stage(nc, M, Q, E, d):
    with stage(nc, "loaded", "summed", "exped", "picked", "turned", "copied", "act_done", "dve_done", "used") as (
            block, loaded, summed, exped, picked, turned, copied, act_done, dve_done, used):
        H, K = PEER_HEADS, TOPK

        def halves(x, half):
            return x.rearrange("p (h s) k -> p h s k", s=2)[:, :, half]

        @block.sync
        def _(sp):
            sp.dma_start(E.iota16[:, :], d["iota16"]).then_inc(loaded, 16)
            sp.dma_start(E.iota128[:, :], d["iota128"]).then_inc(loaded, 16)
            sp.wait_ge(loaded, 32)

        @block.vector
        def _(dve):
            step = Steps(dve, dve_done)
            dve.wait_ge(loaded, 32)
            for b in range(TB):
                for h in range(H):
                    one = Q.sv[:, b, 2 * h, :].unsqueeze(2).broadcast_to([P, K, K])
                    two = Q.sv[:, b, 2 * h + 1, :].unsqueeze(1).broadcast_to([P, K, K])
                    step(dve.tensor_tensor(Q.cand[:, h].rearrange("p (a b) -> p a b", a=K), one, two, ALU.add))
                for h in range(H):
                    top_sixteen(dve, step, Q.cand[:, h], Q.best[:, h], Q.pos[:, h])
                step(dve.tensor_copy(Q.first[:, :], Q.best[:, :, 0]))
                first = Q.first[:, :].unsqueeze(2).broadcast_to([P, H, K])
                step(dve.tensor_tensor(Q.best[:, :, :], Q.best[:, :, :], first, ALU.subtract))
                dve.sem_inc(summed, 1)
                if b:
                    dve.wait_ge(turned, b)
                for half in range(2):
                    if half == 0:
                        step(dve.tensor_scalar(Q.digit[:, :, :], Q.pos[:, :, :], 4, None, ALU.logical_shift_right))
                    else:
                        step(dve.tensor_scalar(Q.digit[:, :, :], Q.pos[:, :, :], 15, None, ALU.bitwise_and))
                    step(dve.tensor_copy(Q.digit_f[:, :], Q.digit[:, :, :].rearrange("p h k -> p (h k)")))
                    step(dve.tensor_tensor(Q.hot[:, :, :], Q.digit_f[:, :].unsqueeze(2).broadcast_to([P, H * K, K]),
                                           E.iota16[:, :].unsqueeze(1).broadcast_to([P, H * K, K]), ALU.is_equal))
                    for h in range(H):
                        num = Q.si[:, b, 2 * h + half, :].unsqueeze(1).broadcast_to([P, K, K])
                        part = Q.hot[:, h * K:(h + 1) * K]
                        step(dve.tensor_tensor(part, part, num, ALU.mult))
                    step(dve.tensor_reduce(Q.pick[:, half], Q.hot[:, :, :], X, ALU.add))
                dve.wait_ge(exped, b + 1)
                step(dve.tensor_reduce(Q.z[:, :], Q.best[:, :, :], X, ALU.add))
                step(dve.reciprocal(Q.z[:, :], Q.z[:, :]))
                step(dve.tensor_tensor(Q.pick[:, 2].rearrange("p (h k) -> p h k", h=H), Q.best[:, :, :],
                                       Q.z[:, :].unsqueeze(2).broadcast_to([P, H, K]), ALU.mult))
                dve.sem_inc(picked, 1)

        @block.scalar
        def _(act):
            step = Steps(act, act_done)
            for b in range(TB):
                act.wait_ge(summed, b + 1)
                step(act.activation(Q.best[:, :, :], Q.best[:, :, :], ACT.Exp))
                act.sem_inc(exped, 1)
                act.wait_ge(turned, b + 1)
                for c in range(3):
                    step(act.copy(E.pickT[:, c, b * P:(b + 1) * P], M.ps[:, c * P:(c + 1) * P]))
                act.sem_inc(copied, 1)

        @block.tensor
        def _(pe):
            for b in range(TB):
                pe.wait_ge(picked, b + 1)
                if b:
                    pe.wait_ge(copied, b)
                for c in range(3):
                    last = pe.transpose(M.ps[:, c * P:(c + 1) * P], Q.pick[:, c], M.ident[:, :])
                last.then_inc(turned, 1)


def spread_stage(nc, M, E, spread_dram):
    G = 8
    with stage(nc, "hots", "hots_used", "laid", "kept", "stored", "stored_seen", "act_done") as (
            block, hots, hots_used, laid, kept, stored, stored_seen, act_done):
        TURNS = P // G

        @block.vector
        def _(dve):
            dve.sem_inc(hots_used, 2)
            with dve.Fori(0, T // G) as g:
                for half in range(2):
                    dve.wait_ge(hots_used, g * 2 + (half + 1))
                    for n in range(4):
                        j = half * 4 + n
                        t = g * G + j
                        dve.tensor_scalar(E.hot_i[:, j], E.iota128[:, :], E.pickT[:, 0, bass.ds(t, 1)], None,
                                          ALU.is_equal).then_inc(hots, 1)
                        dve.tensor_scalar(E.hot_j[:, j], E.iota128[:, :], E.pickT[:, 1, bass.ds(t, 1)],
                                          E.pickT[:, 2, bass.ds(t, 1)], ALU.is_equal, ALU.mult).then_inc(hots, 1)

        @block.tensor
        def _(pe):
            with pe.Fori(0, T // G) as g:
                for half in range(2):
                    pe.wait_ge(hots, g * (2 * G) + (half * G + G))
                    pe.wait_ge(laid, g * 2 + (half + 1))
                    for n in range(4):
                        j = half * 4 + n
                        last = pe.matmul(M.ps[:, half * BANK + n * P:half * BANK + (n + 1) * P], E.hot_i[:, j],
                                         E.hot_j[:, j], start=True, stop=True)
                    last.then_inc(hots_used, 1)

        @block.scalar
        def _(act):
            step = Steps(act, act_done)
            act.sem_inc(laid, 2)
            with act.Fori(0, TB) as b:
                act.wait_ge(kept, b + 1)
                with act.Fori(0, TURNS) as g:
                    for half in range(2):
                        act.wait_ge(hots_used, b * (2 * TURNS) + (g * 2 + (half + 3)))
                        step.hold(laid)
                        at = g * G + half * 4
                        step(act.copy(E.table[:, :, bass.ds(at, 4)],
                                      bank(M.ps, half).rearrange("p (t j) -> p j t", t=4)))
                        act.sem_inc(laid, 1)
                    step.again()
                act.sem_inc(stored, 1)

        @block.sync
        def _(sp):
            sp.sem_inc(kept, 1)
            with sp.Fori(0, TB) as b:
                sp.wait_ge(stored, b + 1)
                sp.dma_start(spread_dram.rearrange("j i t -> i j t")[:, :, bass.ds(b * P, P)],
                             E.table[:, :, :]).then_inc(stored_seen, 16)
                sp.wait_ge(stored_seen, b * 16 + 16)
                sp.sem_inc(kept, 1)


def block_two(nc, M, d):
    def mod(i, c=0):
        return M.mod[:, i * KB:(i + 1) * KB, c]

    with ExitStack() as ctx:
        def sb(name, *shape, dt=F32, of=ctx):
            return of.enter_context(nc.sbuf_tensor(name, [P, *shape], dt))

        M.cols2, M.ctx = sb("cols2", NCOLS2), sb("context", KB, CTX)
        M.gate_row = sb("gate_row", 16)
        M.cos2, M.sin2, M.rot2 = sb("cos2", TA), sb("sin2", TA), sb("rot2", P)
        M.sel, M.decay_mask, M.starts = sb("sel", 8, P), sb("decay_mask", 2, T), sb("starts", TA)
        M.csig2, M.cond2, M.g_qn = sb("csig2", 16), sb("cond2", KB, 2), sb("g_qn_s", 2)
        conditions_stage(nc, M, d)
        ada_stage(nc, M, d["w_ada2"], 0, M.cond2, 2, cols2(M, "ada_b"), M.mod)
        norm_part(nc, M, lambda k: M.ctx[:, k], CTX, KB, cols2(M, "g1"), mod(1, 1), mod(0, 1),
                  lambda k: M.h[:, k, 0:CTX])
        norm_part(nc, M, lambda k: M.x[:, k], T, KB, cols2(M, "g1"), mod(1), mod(0),
                  lambda k: M.h[:, k, CTX:TA].rearrange("p (l r) -> p r l", r=4))
        with ExitStack() as mixer:
            N, R, Z = Named(), Named(), Named()
            N.mix = sb("mix", KB, T, of=mixer)
            N.o = sb("o", 4, T, of=mixer)
            N.v, N.gates = sb("ml_v", AB, 512, of=mixer), sb("ml_gates", AB, 16, of=mixer)
            raw = ExitStack()
            N.mq_raw, N.mk_raw = sb("mq_raw", 2, T + 2, of=raw), sb("mk_raw", 2, TA + 4, of=raw)
            with ExitStack() as inner:
                N.cq, N.ckv, N.kr = sb("cq", 2, T, of=inner), sb("ckv", TA, of=inner), sb("kr", TA, of=inner)
                with ExitStack() as weights:
                    N.wv, N.wkr, N.wg = (sb("wv", KB, 512, of=weights), sb("wkr", KB, 64, of=weights),
                                         sb("wg", KB, 16, of=weights))
                    project_stage(nc, M, N, d)
                free = M.h[:, :, :].rearrange("p k t -> p (k t)").rearrange("p (n t) -> p n t", t=TA)
                N.sqk, N.lnk, N.rk, R.sq, R.sqr, R.kn, R.tmp, R.kr = (free[:, n] for n in range(8))
                N.work = R.tmp
                latent_norm_stage(nc, M, N)
                R.w = sb("mla_w", 640, of=inner)
                R.qn, R.qr = sb("r_qn", T, of=inner), sb("r_qr", T, of=inner)
                spare = M.ring[:, :, :].rearrange("p j n -> p (j n)")
                R.v = spare[:, 0:TA].rearrange("p (b d) -> p b d", b=AB)
                R.p = spare[:, TA:3 * TA].rearrange("p (b t) -> p b t", b=2)
                R.pT = spare[:, 3 * TA:5 * TA].rearrange("p (b t) -> p b t", b=2)
                R.peak, R.z, R.rz = sb("r_peak", 2, of=inner), sb("r_z", 2, of=inner), sb("r_rz", 1, of=inner)
                mla_stage(nc, M, N, R, d)
            with ExitStack() as inner:
                N.mq, N.mk = sb("mq", 2, T, of=inner), sb("mk", 2, TA, of=inner)
                N.rows = M.h[:, :, :].rearrange("p k t -> p (k t)").rearrange("p (n t) -> p n t", t=TA)[:, 0:6]
                spare = M.ring[:, :, :].rearrange("p j n -> p (j n)").rearrange("p (n t) -> p n t", t=T)
                N.nat, N.tot = sb("nat", 6, TA, of=inner), sb("tot", AB, of=inner)
                N.dcol, N.totb = sb("dcol", 2, AB, 4, of=inner), sb("totb", 8, AB, of=inner)
                Z.bias, N.fabs = sb("bias", 8, AB, AB, of=inner), sb("fabs", AB, 8, of=inner)
                N.conv, N.conv_sig = spare[:, 0:2], spare[:, 2:4]
                conv_stage(nc, M, N)
                decay_stage(nc, M, N, Z)
                Z.a, Z.am, Z.em, Z.den = (spare[:, n] for n in range(4))
                Z.e, Z.w, Z.hs, Z.lns = spare[:, 4:6], spare[:, 6:8], spare[:, 8:12], spare[:, 12:16]
                mlstm_stage(nc, M, N, Z)
                mlstm_out_stage(nc, M, N, Z)
            raw.close()
            residual_stage(nc, M, d["w_out2"], 0, N.mix, mod(2), True)
    M.h = M.h[:, :, 0:T]
    norm_part(nc, M, lambda k: M.x[:, k], T, KB, M.g2[:, :], mod(4), mod(3), lambda k: M.h[:, k])
    Q, E = Named(), Named()
    spread_dram = nc.dram_tensor("expert_weights", (NKEYS, P, T), F32, kind="Internal").ap()
    with ExitStack() as ctx:
        def sb(name, *shape, dt=F32, of=ctx):
            return of.enter_context(nc.sbuf_tensor(name, [P, *shape], dt))

        E.iota16, E.iota128, E.pickT = sb("iota16", 16), sb("iota128", P), sb("pickT", 3, T)
        with ExitStack() as inner:
            HP = 2 * PEER_HEADS
            Q.keys, Q.q, Q.s = sb("sub_keys", 2, P, of=inner), sb("p_q", 2, T, of=inner), sb("p_s", 2, TB, P, of=inner)
            Q.top, Q.at = sb("p_top", TB, TOPK, of=inner), sb("p_at", TB, TOPK, dt=U32, of=inner)
            Q.sv, Q.si = sb("p_sv", TB, HP, TOPK, of=inner), sb("p_si", TB, HP, TOPK, of=inner)
            query_stage(nc, M, Q, d["w_pq"], d["sub_keys"])
            Q.cand, Q.best = sb("p_cand", 8, 256, of=inner), sb("p_best", 8, TOPK, of=inner)
            Q.pos, Q.digit = sb("p_pos", 8, TOPK, dt=U32, of=inner), sb("p_digit", 8, TOPK, dt=U32, of=inner)
            Q.digit_f, Q.hot = sb("p_digit_f", P, of=inner), sb("p_hot", P, TOPK, of=inner)
            Q.pick, Q.z, Q.first = sb("p_pick", 3, P, of=inner), sb("p_z", 8, of=inner), sb("p_first", 8, of=inner)
            choice_stage(nc, M, Q, E, d)
        with ExitStack() as inner:
            E.hot_i, E.hot_j = sb("hot_i", 8, P, of=inner), sb("hot_j", 8, P, of=inner)
            E.table = sb("table", P, P, of=inner)
            spread_stage(nc, M, E, spread_dram)
    M.ring_place.close()
    with ExitStack() as ctx:
        E = split_places(nc, ctx, "experts", 4)
        E.raw_u = ctx.enter_context(nc.sbuf_tensor("raw_u", [P, 4, D], F32))
        E.raw_v = M.scratch[:, 0:8].rearrange("p t n -> p (t n)").rearrange("p (j n) -> p j n", j=4)
        E.act = M.scratch[:, 8:12]
        gated_mlp_stage(nc, M, E, d["u_tiles"], d["v_tiles"], 0, NKEYS // 4, ACT.Gelu,
                        spread_dram.rearrange("(g j) i t -> g i j t", j=4))


def output_stage(nc, M, out):
    with stage(nc, "stored") as (block, stored):
        @block.sync
        def _(sp):
            sp.dma_start(out, M.x[:, :, :]).then_inc(stored, 16)
            sp.wait_ge(stored, 16)


def build(nc, d, out):
    with ExitStack() as ctx:
        def sb(name, *shape, dt=F32):
            return ctx.enter_context(nc.sbuf_tensor(name, [P, *shape], dt))

        M = Named()
        M.ps = ctx.enter_context(nc.psum_tensor("ps", [P, 8 * BANK], F32))
        M.x, M.h = sb("x", KB, T), sb("h", KB, TA)
        M.ident, M.ones, M.bd64, M.rot = sb("ident", P), sb("ones", P), sb("bd64", P), sb("rot", P)
        M.eps, M.inv_freq = sb("eps", 1), sb("inv_freq", 1)
        M.pos = sb("pos", T, dt=I32)
        M.scratch = sb("scratch", 12, T)
        M.cos, M.sin, M.ln, M.rstd, M.tmp, M.tmp2 = (M.scratch[:, n] for n in range(6))
        M.sq, M.rstd2, M.qkn = (M.scratch[:, n:n + 2] for n in (6, 8, 10))
        M.gs = sb("gs", KB)
        M.cond, M.csig = sb("cond", KB, 1), sb("csig", KB, 1)
        M.cols, M.mod = sb("cols", NCOLS), sb("mod", 48, 2)
        M.gain_a, M.gain_b, M.subln, M.nlam = sb("gain_as", 2), sb("gain_bs", 2), sb("subln_s", 1), sb("nlam", 1)
        M.gate_bias = sb("gate_bias_s", 16)
        M.g2 = sb("g2", KB)
        M.ring_place = ctx.enter_context(ExitStack())
        M.ring = M.ring_place.enter_context(nc.sbuf_tensor("ring", [P, 9, KB * P], F32))
        full_h = M.h
        M.h = full_h[:, :, 0:T]
        setup_stage(nc, M, d)
        block_one(nc, M, d)
        M.h = full_h
        block_two(nc, M, d)
        output_stage(nc, M, out)



def tiles(w):
    k, m = w.shape
    return w.reshape(k // P, P, m // P, P).transpose(2, 1, 0, 3).reshape(m // P, P, k)


def row_tiles(w):
    k, m = w.shape
    return w.reshape(k // P, P, m // 1024, 1024).transpose(2, 0, 1, 3).reshape(-1, P, 1024)


def columns(v):
    return v.reshape(-1, P).T


def layout_one(a):
    f32 = np.float32
    L = {}
    perm = np.arange(T).reshape(P, 4).T.reshape(T)
    L["x"] = a["x"][0][perm].T.reshape(KB, P, T).transpose(1, 0, 2)
    L["positions"] = np.broadcast_to(a["positions"][0][perm][None, :], (P, T))
    L["c"] = columns(a["c"][0])[:, :, None]
    L["ident"] = np.eye(P, dtype=f32)
    L["ones"] = np.ones((P, P), f32)
    L["bd64"] = np.kron(np.eye(2), np.ones((64, 64))).astype(f32)
    rot = np.zeros((P, P), f32)
    freq = np.zeros((P, 1), f32)
    for h in range(2):
        for i in range(8):
            rot[h * 64 + i + 8, h * 64 + i] = -1.0
            rot[h * 64 + i, h * 64 + i + 8] = 1.0
            freq[h * 64 + i] = freq[h * 64 + i + 8] = 500000.0 ** (-2 * i / 16)
    L["rot"], L["inv_freq"] = rot, freq
    L["eps"] = np.full((P, 1), EPS, f32)
    r, l = np.arange(T) // P, np.arange(T) % P
    tok = 4 * l + r
    mask = np.full((P, TB, T + 2 * P), NEG, f32)
    for b in range(TB):
        q = tok[b * P:(b + 1) * P]
        mask[:, b, 0:T][np.abs(q[:, None] - tok[None, :]) <= 64] = 0.0
        d = q[:, None] - q[None, :]
        mask[:, b, T:T + P][np.abs(d) <= 64 * 4] = 0.0
        mask[:, b, T + P:][(d % 16 == 0) & (np.abs(d) <= 64 * 16)] = 0.0
    L["mask"] = mask
    cols, wa, wb, wg = [], [], [], []
    for i in range(DEPTH):
        lam = np.zeros((P, 4), f32)
        lam[0:64] = a["lambda_a"][i].T
        init = 0.8 - 0.6 * np.exp(-0.3 * i)
        parts = {"ada_b": columns(a["ada_b"][i]), "g_mix": columns(a["norm_mix_g"][i]),
                 "g_mlp": columns(a["norm_mlp_g"][i]), "gate_bias": columns(a["gate_bias"][i]),
                 "gain_a": np.tile(a["qk_gain_a"][i].T, (2, 1)), "gain_b": np.tile(a["qk_gain_b"][i].T, (2, 1)),
                 "subln": columns(a["subln_g_a"][i]), "lam": lam,
                 "lam_init": np.broadcast_to(np.array([init, 1 - init], f32), (P, 2))}
        cols.append(np.concatenate([parts[n] for n in COLS], axis=1))
        w = tiles(a["w_in"][i])
        wa.append(np.stack([w[h + 8 * c] for h in range(8) for c in range(3)]))
        wb.append(np.stack([w[24 + 6 * c + 2 * g + pair] for pair in range(2) for g in range(3) for c in range(3)]))
        br = tiles(a["w_branch_a"][i])
        wg.append(np.stack([t for m in range(8) for t in (w[42 + m], w[50 + m], br[m])]))
    L["cols"] = np.stack(cols)
    L["w_a"], L["w_b"], L["w_gate"] = (np.concatenate(t) for t in (wa, wb, wg))
    L["w_branch_b"] = np.stack([tiles(w).transpose(1, 0, 2).reshape(P, KB, 2, P) for w in a["w_branch_b"]])
    L["w_ada"] = np.concatenate([row_tiles(w) for w in a["ada_w"]])
    L["w_out"] = np.concatenate([tiles(w) for w in a["w_out"]])
    L["w_up"] = np.concatenate([tiles(w) for w in a["w_mlp_up"]])
    L["w_down"] = np.concatenate([w.reshape(FB // 4, 4, P, D).transpose(0, 2, 1, 3) for w in a["w_mlp_down"]])
    return L


def layout_two(a):
    f32 = np.float32
    L = {}
    a = {k[:-2]: v for k, v in a.items() if k.endswith("_2")}
    gain = {n: a[n][0] for n in ("g_norm1", "g_norm2", "g_cq", "g_ckv", "g_qn", "g_kn", "g_mlstm")}

    def padded(v):
        out = np.zeros((P, 2), f32)
        out[:, 0], out[0:64, 1] = v[0:P], v[P:]
        return out

    parts = {"ada_b": columns(a["b_ada"][0]), "g1": columns(gain["g_norm1"]), "g2": columns(gain["g_norm2"]),
             "c": np.stack([columns(a["c"][0]), columns(a["c_ctx"])], axis=2).reshape(P, 16),
             "g_cq": columns(gain["g_cq"]), "g_ckv": columns(gain["g_ckv"]), "g_qn": padded(gain["g_qn"]),
             "g_kn": padded(gain["g_kn"]),
             "conv": a["conv_qk"][0].reshape(3, 4, P).transpose(2, 0, 1).reshape(P, 12),
             "g_ml": columns(gain["g_mlstm"])}
    L["cols2"] = np.concatenate([parts[n] for n in COLS2], axis=1)
    L["g2"] = parts["g2"]
    L["ctx"] = a["ctx"][0].T.reshape(KB, P, CTX).transpose(1, 0, 2)
    row = np.concatenate([a["b_igate"][0].reshape(8), a["b_fgate"][0].reshape(8)])
    L["gate_row"] = np.broadcast_to(row[None], (P, 16))
    w = a["w_in"][0]
    order = [(0, 256), (256, 384), (448, 704), (704, 960), (1472, 1984)]
    L["w_in2"] = tiles(np.concatenate([w[:, lo:hi] for lo, hi in order], axis=1))
    L["w_kr"] = w[:, 384:448].reshape(KB, P, 64).transpose(1, 0, 2)
    L["w_v2"] = w[:, 960:1472].reshape(KB, P, 512).transpose(1, 0, 2)
    L["w_g2"] = w[:, 1984:2000].reshape(KB, P, 16).transpose(1, 0, 2)
    uq = a["w_uq"][0].reshape(2, P, MLA_HEADS, 192)
    ukv = a["w_ukv"][0].reshape(P, MLA_HEADS, 256)
    L["w_mla"] = np.stack([np.concatenate([uq[0, :, h], uq[1, :, h], ukv[:, h]], axis=1) for h in range(MLA_HEADS)])
    L["w_ada2"], L["w_out2"], L["w_pq"] = row_tiles(a["w_ada"][0]), tiles(a["w_out"][0]), tiles(a["w_pq"][0])
    L["sub_keys"] = a["sub_keys"][0].reshape(16, NKEYS, P).transpose(0, 2, 1)
    L["u_tiles"] = a["expert_u"][0].reshape(P, NKEYS, KB, P).transpose(1, 3, 2, 0).reshape(NKEYS, P, D)
    L["v_tiles"] = a["expert_v"][0].reshape(P, 32, 4, D).transpose(1, 0, 2, 3)
    inv = 10000.0 ** (-np.arange(16, dtype=f32) * (2.0 / 32))
    cos, sin = np.ones((P, TA), f32), np.zeros((P, TA), f32)
    pos = np.arange(T)
    for base, p in ((0, pos // 64), (32, pos % 64)):
        ang = p.astype(f32)[None, :] * inv.astype(f32)[:, None]
        for half in range(2):
            cos[base + 16 * half:base + 16 * half + 16, CTX:] = np.cos(ang)
            sin[base + 16 * half:base + 16 * half + 16, CTX:] = np.sin(ang)
    L["cos2"], L["sin2"] = cos, sin
    rot = np.zeros((P, P), f32)
    for base in (0, 32):
        for i in range(16):
            rot[base + i + 16, base + i] = -1.0
            rot[base + i, base + i + 16] = 1.0
    L["rot2"] = rot
    sel = np.zeros((P, 8, P), f32)
    for c in range(8):
        sel[c // 4 * 32 + c % 4, c] = 1.0
    L["sel"] = sel
    s, t = np.arange(P)[:, None], np.arange(P)[None, :]
    L["decay_mask"] = np.stack([np.tile(np.where(s <= t, 0, NEG), (1, 4)), np.tile(np.where(s >= t, 0, NEG), (1, 4))],
                               axis=1).astype(f32)
    L["starts"] = np.broadcast_to((np.arange(TA) % P != 0).astype(f32)[None], (P, TA))
    L["iota16"] = np.broadcast_to(np.arange(16, dtype=f32)[None], (P, 16))
    L["iota128"] = np.broadcast_to(np.arange(P, dtype=f32)[None], (P, P))
    return L


def kernel(**inputs):
    import concourse.bacc as bacc
    from concourse.bass_utils import run_bass_kernel_spmd

    a = {k: np.asarray(v) for k, v in inputs.items()}
    L = layout_one(a)
    L.update(layout_two(a))
    L = {k: np.ascontiguousarray(v) for k, v in L.items()}
    nc = bacc.Bacc("TRN2", target_bir_lowering=False, num_devices=1)
    d = {k: nc.dram_tensor(f"in_{k}", v.shape, mybir.dt.from_np(v.dtype), kind="ExternalInput").ap()
         for k, v in L.items()}
    out = nc.dram_tensor("out", (P, KB, T), F32, kind="ExternalOutput").ap()
    build(nc, d, out)
    r = run_bass_kernel_spmd(nc, [{f"in_{k}": v for k, v in L.items()}], core_ids=[0])
    y = r.results[0]["out"]
    return y.transpose(2, 1, 0).reshape(4, P, D).transpose(1, 0, 2).reshape(1, T, D)
```
